# Optimizing a Trainium2 kernel written in Bass

```python
import jax, jax.numpy as jnp
from jax import lax
import numpy as np

D_MODEL = 1024
BATCH = 1
SEQ = 1024
DEPTH = 1

N_MIXERS = 3
RMS_EPS = 1e-6
BLOCK = 128
NEG = -1e30

SWA_HEAD_DIM = 64
SWA_HEADS = D_MODEL // SWA_HEAD_DIM
SWA_KV_HEADS = SWA_HEADS // 8
SWA_GROUP = SWA_HEADS // SWA_KV_HEADS
WINDOW = 128

SB_HEAD_DIM = 64
SB_HEADS = D_MODEL // SB_HEAD_DIM

RET_QK_DIM = 256
RET_HEADS = D_MODEL // RET_QK_DIM
RET_V_DIM = 2 * RET_QK_DIM

D_FF = 4 * D_MODEL

N_A = len(range(0, DEPTH, N_MIXERS))
N_B = len(range(1, DEPTH, N_MIXERS))
N_C = len(range(2, DEPTH, N_MIXERS))


def rms_norm(x, g):
    xf = x.astype(jnp.float32)
    y = xf * lax.rsqrt(jnp.mean(xf * xf, axis=-1, keepdims=True) + RMS_EPS)
    return (y * g.astype(jnp.float32)).astype(x.dtype)

def alibi_slopes(n_heads):
    return jnp.exp2(-8.0 * jnp.arange(1, n_heads + 1, dtype=jnp.float32) / n_heads)

def swa_mixer(h, w_qkv, sinks, w_o):
    B_, T, _ = h.shape
    nb = T // BLOCK
    HD, KV, G = SWA_HEAD_DIM, SWA_KV_HEADS, SWA_GROUP
    qkv = h @ w_qkv
    q, k, v = jnp.split(qkv, [SWA_HEADS * HD, (SWA_HEADS + KV) * HD], axis=-1)
    q = q.reshape(B_, nb, BLOCK, KV, G, HD)
    k = k.reshape(B_, nb, BLOCK, KV, HD)
    v = v.reshape(B_, nb, BLOCK, KV, HD)

    def with_prev(a):
        prev = jnp.pad(a, ((0, 0), (1, 0), (0, 0), (0, 0), (0, 0)))[:, :-1]
        return jnp.concatenate([prev, a], axis=2)

    kb, vb = with_prev(k), with_prev(v)
    s = jnp.einsum('bnqkgd,bnskd->bnkgqs', q, kb).astype(jnp.float32) * (HD ** -0.5)

    blk = jnp.arange(nb)[:, None, None]
    qi = jnp.arange(BLOCK)[None, :, None]
    kj = jnp.arange(2 * BLOCK)[None, None, :]
    dist = BLOCK + qi - kj
    kpos = (blk - 1) * BLOCK + kj
    mask = (dist >= 0) & (dist < WINDOW) & (kpos >= 0)
    slopes = alibi_slopes(SWA_HEADS).reshape(1, 1, KV, G, 1, 1)
    bias = -slopes * dist.astype(jnp.float32)[None, :, None, None]
    logits = jnp.where(mask[None, :, None, None], s + bias, NEG)

    sink = sinks.astype(jnp.float32).reshape(1, 1, KV, G, 1, 1)
    m = jnp.maximum(jnp.max(logits, axis=-1, keepdims=True), sink)
    p = jnp.exp(logits - m)
    probs = p / (jnp.sum(p, axis=-1, keepdims=True) + jnp.exp(sink - m))
    o = jnp.einsum('bnkgqs,bnskd->bnqkgd', probs.astype(vb.dtype), vb)
    return o.reshape(B_, T, SWA_HEADS * HD) @ w_o

def stick_breaking_mixer(h, w_qkv, w_o):
    B_, T, _ = h.shape
    HD, H = SB_HEAD_DIM, SB_HEADS
    qkv = (h @ w_qkv).reshape(B_, T, 3, H, HD)
    q = jnp.transpose(qkv[:, :, 0], (0, 2, 1, 3))
    k = jnp.transpose(qkv[:, :, 1], (0, 2, 1, 3))
    v = jnp.transpose(qkv[:, :, 2], (0, 2, 1, 3))
    scale = HD ** -0.5
    outs = []
    for n in range(T // BLOCK):
        q0, end = n * BLOCK, (n + 1) * BLOCK
        z = jnp.einsum('bhqd,bhsd->bhqs', q[:, :, q0:end], k[:, :, :end]).astype(jnp.float32) * scale
        t_pos = q0 + jnp.arange(BLOCK)[:, None]
        s_pos = jnp.arange(end)[None, :]
        causal = (s_pos < t_pos)[None, None]
        log_beta = jax.nn.log_sigmoid(z)
        log_1m_beta = jnp.where(causal, jax.nn.log_sigmoid(-z), 0.0)
        rest = lax.cumsum(log_1m_beta, axis=3, reverse=True) - log_1m_beta
        a = jnp.where(causal, jnp.exp(log_beta + rest), 0.0)
        outs.append(jnp.einsum('bhqs,bhsd->bhqd', a.astype(v.dtype), v[:, :, :end]))
    o = jnp.concatenate(outs, axis=2)
    return jnp.transpose(o, (0, 2, 1, 3)).reshape(B_, T, H * HD) @ w_o

def retention_mixer(h, w_in, w_o):
    B_, T, _ = h.shape
    nc, C, H, dk, dv = T // BLOCK, BLOCK, RET_HEADS, RET_QK_DIM, RET_V_DIM
    proj = h @ w_in
    q, k, v, g = jnp.split(proj, [H * dk, 2 * H * dk, 2 * H * dk + H * dv], axis=-1)
    q = q.astype(jnp.float32).reshape(B_, nc, C, H, dk)
    k = k.astype(jnp.float32).reshape(B_, nc, C, H, dk) * (dk ** -0.5)
    v = v.astype(jnp.float32).reshape(B_, nc, C, H, dv)

    log_gamma = jnp.log1p(-jnp.exp2(-5.0 - jnp.arange(H, dtype=jnp.float32)))
    idx = jnp.arange(C)
    diff = idx[:, None] - idx[None, :]
    decay_mat = jnp.where(diff >= 0,
                          jnp.exp(log_gamma[:, None, None] * jnp.maximum(diff, 0).astype(jnp.float32)),
                          0.0)
    scores = jnp.einsum('bnihd,bnjhd->bnhij', q, k) * decay_mat
    o_inner = jnp.einsum('bnhij,bnjhe->bnihe', scores, v)
    q_decay = jnp.exp(log_gamma[:, None] * (idx + 1).astype(jnp.float32))
    k_decay = jnp.exp(log_gamma[:, None] * (C - 1 - idx).astype(jnp.float32))
    chunk_decay = jnp.exp(log_gamma * C)[None, :, None, None]
    kv_chunk = jnp.einsum('bnjhd,hj,bnjhe->bnhde', k, k_decay, v)

    def step(state, kv_n):
        return state * chunk_decay + kv_n, state

    init = jnp.zeros((B_, H, dk, dv), jnp.float32)
    _, prev_states = lax.scan(step, init, jnp.moveaxis(kv_chunk, 1, 0))
    prev_states = jnp.moveaxis(prev_states, 0, 1)
    o_cross = jnp.einsum('bnihd,hi,bnhde->bnihe', q, q_decay, prev_states)
    o = o_inner + o_cross
    o = o * lax.rsqrt(jnp.mean(o * o, axis=-1, keepdims=True) + RMS_EPS)
    o = o.reshape(B_, T, H * dv)
    y = jax.nn.silu(g.astype(jnp.float32)) * o
    return y.astype(h.dtype) @ w_o

def squared_relu_mlp(h, w_up, w_down):
    a = jax.nn.relu(h @ w_up)
    return (a * a) @ w_down

def first_inputs(seed: int = 0) -> dict:
    key = jax.random.key(seed)
    ks = jax.random.split(key, 16)

    def dense(k, shape):
        return jax.random.normal(k, shape, jnp.float32) * (shape[-2] ** -0.5)

    def gain(k, shape):
        return 1.0 + 0.02 * jax.random.normal(k, shape, jnp.float32)

    swa_qkv_dim = (SWA_HEADS + 2 * SWA_KV_HEADS) * SWA_HEAD_DIM
    ret_in_dim = 2 * RET_HEADS * RET_QK_DIM + 2 * RET_HEADS * RET_V_DIM
    return {
        "x": jax.random.normal(ks[0], (BATCH, SEQ, D_MODEL), jnp.float32),
        "attn_norm": gain(ks[1], (DEPTH, D_MODEL)),
        "mlp_norm": gain(ks[2], (DEPTH, D_MODEL)),
        "final_norm": gain(ks[3], (D_MODEL,)),
        "swa_w_qkv": dense(ks[4], (N_A, D_MODEL, swa_qkv_dim)),
        "swa_sinks": 0.5 * jax.random.normal(ks[5], (N_A, SWA_HEADS), jnp.float32),
        "swa_w_o": dense(ks[6], (N_A, SWA_HEADS * SWA_HEAD_DIM, D_MODEL)),
        "sb_w_qkv": dense(ks[7], (N_B, D_MODEL, 3 * SB_HEADS * SB_HEAD_DIM)),
        "sb_w_o": dense(ks[8], (N_B, SB_HEADS * SB_HEAD_DIM, D_MODEL)),
        "ret_w_in": dense(ks[9], (N_C, D_MODEL, ret_in_dim)),
        "ret_w_o": dense(ks[10], (N_C, RET_HEADS * RET_V_DIM, D_MODEL)),
        "mlp_w_up": dense(ks[11], (DEPTH, D_MODEL, D_FF)),
        "mlp_w_down": dense(ks[12], (DEPTH, D_FF, D_MODEL)),
    }

def first_block(x, attn_norm, mlp_norm, final_norm, swa_w_qkv, swa_sinks, swa_w_o,
              sb_w_qkv, sb_w_o, ret_w_in, ret_w_o, mlp_w_up, mlp_w_down):
    h = x
    for i in range(DEPTH):
        kind, j = i % N_MIXERS, i // N_MIXERS
        u = rms_norm(h, attn_norm[i])
        if kind == 0:
            mix = swa_mixer(u, swa_w_qkv[j], swa_sinks[j], swa_w_o[j])
        elif kind == 1:
            mix = stick_breaking_mixer(u, sb_w_qkv[j], sb_w_o[j])
        else:
            mix = retention_mixer(u, ret_w_in[j], ret_w_o[j])
        h = h + mix
        h = h + squared_relu_mlp(rms_norm(h, mlp_norm[i]), mlp_w_up[i], mlp_w_down[i])
    return rms_norm(h, final_norm)


DEPTH_2 = 2

GRID_W = 64
CTX_LEN = 256
EPS = 1e-6
A_WIDTH = D_MODEL // 2
A_CONV_W = 31
B_GROUPS = 4
B_WIDTH = D_MODEL // 2
B_GROUP_DIM = B_WIDTH // B_GROUPS
C_WIDTH = D_MODEL // 2
C_CONV_W = 3
HEAD_DIM = 64
N_Q_HEADS = (D_MODEL // 2) // HEAD_DIM
N_KV_HEADS = max(N_Q_HEADS // 4, 1)
Q_GROUP = N_Q_HEADS // N_KV_HEADS
ATT_WIDTH = N_Q_HEADS * HEAD_DIM
KV_WIDTH = N_KV_HEADS * HEAD_DIM
ROPE_BASE = 10000.0
NEG_INF = -1e30
EVEN_IN = 3 * A_WIDTH + 2 * B_WIDTH
EVEN_MIX = A_WIDTH + B_WIDTH
ODD_IN = 4 * C_WIDTH + 2 * ATT_WIDTH + 2 * KV_WIDTH
ODD_MIX = C_WIDTH + ATT_WIDTH


def _rmsnorm(x, g):
    xf = x.astype(jnp.float32)
    y = xf * lax.rsqrt(jnp.mean(xf * xf, axis=-1, keepdims=True) + EPS)
    return (y * g.astype(jnp.float32)).astype(x.dtype)

def _layernorm(x, g, b):
    xf = x.astype(jnp.float32)
    mu = jnp.mean(xf, axis=-1, keepdims=True)
    var = jnp.mean(jnp.square(xf - mu), axis=-1, keepdims=True)
    y = (xf - mu) * lax.rsqrt(var + EPS)
    return (y * g.astype(jnp.float32) + b.astype(jnp.float32)).astype(x.dtype)

def _split(t, widths):
    cuts, acc = [], 0
    for w in widths[:-1]:
        acc += w
        cuts.append(acc)
    return jnp.split(t, cuts, axis=-1)

def _modulation(cvec, w_mod, b_mod):
    h = jax.nn.silu(cvec) @ w_mod + b_mod
    shift, scale, gate = jnp.split(h[:, None, :], 3, axis=-1)
    return shift, scale, gate

def _pre(x, g, shift, scale):
    return _rmsnorm(x, g) * (1 + scale) + shift

def _dwconv(u, w):
    pad = (w.shape[0] - 1) // 2
    return lax.conv_general_dilated(
        u, w[:, None, :].astype(u.dtype), window_strides=(1,), padding=[(pad, pad)],
        dimension_numbers=('NWC', 'WIO', 'NWC'), feature_group_count=u.shape[-1])

def _fourier_mix(v, fw):
    b, l, _ = v.shape
    vg = v.reshape(b, l, B_GROUPS, B_GROUP_DIM).astype(jnp.float32)
    f = jnp.fft.fftn(vg, axes=(1, 3), norm='ortho').real.astype(v.dtype)
    return jnp.einsum('blgd,gde->blge', f, fw).reshape(b, l, B_WIDTH)

def _even_mix(h, w_in, a_conv_w, a_conv_b, a_ln_g, a_ln_b, a_pw_w, a_pw_b, b_fw, w_out):
    a_val, a_glu, a_gate, b_val, b_gate = _split(h @ w_in, [A_WIDTH, A_WIDTH, A_WIDTH, B_WIDTH, B_WIDTH])
    u = a_val * jax.nn.sigmoid(a_glu)
    u = jax.nn.silu(_layernorm(_dwconv(u, a_conv_w) + a_conv_b, a_ln_g, a_ln_b))
    y_a = (u @ a_pw_w + a_pw_b) * jax.nn.silu(a_gate)
    y_b = _fourier_mix(b_val, b_fw) * jax.nn.silu(b_gate)
    return jnp.concatenate([y_a, y_b], axis=-1) @ w_out

def _rope_tables(row, col):
    nf = HEAD_DIM // 4
    inv = jnp.power(ROPE_BASE, -jnp.arange(nf, dtype=jnp.float32) / nf)
    ang = jnp.stack([row.astype(jnp.float32)[:, None] * inv,
                     col.astype(jnp.float32)[:, None] * inv], axis=1)
    return jnp.cos(ang), jnp.sin(ang)

def _apply_rope(t, cos, sin):
    b, l, h, d = t.shape
    tr = t.astype(jnp.float32).reshape(b, l, h, 2, 2, d // 4)
    t1, t2 = tr[..., 0, :], tr[..., 1, :]
    cs, sn = cos[None, :, None], sin[None, :, None]
    out = jnp.stack([t1 * cs - t2 * sn, t2 * cs + t1 * sn], axis=-2)
    return out.reshape(b, l, h, d).astype(t.dtype)

def _sink_softmax(logits, sink):
    m = sink
    for s in logits:
        m = jnp.maximum(m, jnp.max(s, axis=-1, keepdims=True))
    ps = [jnp.exp(s - m) for s in logits]
    denom = jnp.exp(sink - m)
    for p in ps:
        denom = denom + jnp.sum(p, axis=-1, keepdims=True)
    return [p / denom for p in ps]

def _window_attention(q, k, v, kc, vc, sink):
    b, l, hq, hd = q.shape
    nb = l // BLOCK
    scale = HEAD_DIM ** -0.5
    qb = q.reshape(b, nb, BLOCK, N_KV_HEADS, Q_GROUP, hd)

    def band(t):
        tp = jnp.pad(t, ((0, 0), (BLOCK, BLOCK), (0, 0), (0, 0))).reshape(b, nb + 2, BLOCK, N_KV_HEADS, hd)
        return jnp.concatenate([tp[:, :-2], tp[:, 1:-1], tp[:, 2:]], axis=2)

    kw, vw = band(k), band(v)
    qpos = jnp.arange(l).reshape(nb, BLOCK)
    kpos = jnp.arange(-BLOCK, l + BLOCK).reshape(nb + 2, BLOCK)
    kwpos = jnp.concatenate([kpos[:-2], kpos[1:-1], kpos[2:]], axis=1)
    valid = ((jnp.abs(qpos[:, :, None] - kwpos[:, None, :]) <= WINDOW)
             & (kwpos >= 0)[:, None, :] & (kwpos < l)[:, None, :])
    s_win = jnp.einsum('bnqhgd,bnkhd->bnhgqk', qb, kw).astype(jnp.float32) * scale
    s_win = jnp.where(valid[None, :, None, None], s_win, NEG_INF)
    s_ctx = jnp.einsum('bnqhgd,bchd->bnhgqc', qb, kc).astype(jnp.float32) * scale
    sink_b = sink.astype(jnp.float32).reshape(N_KV_HEADS, Q_GROUP)[None, None, :, :, None, None]
    p_win, p_ctx = _sink_softmax([s_win, s_ctx], sink_b)
    o = (jnp.einsum('bnhgqk,bnkhd->bnqhgd', p_win.astype(v.dtype), vw)
         + jnp.einsum('bnhgqc,bchd->bnqhgd', p_ctx.astype(v.dtype), vc))
    return o.reshape(b, l, hq * hd)

def _context_attention(q, k, v, sink):
    b, lc, hq, hd = q.shape
    qg = q.reshape(b, lc, N_KV_HEADS, Q_GROUP, hd)
    s = jnp.einsum('bqhgd,bkhd->bhgqk', qg, k).astype(jnp.float32) * (HEAD_DIM ** -0.5)
    sink_b = sink.astype(jnp.float32).reshape(N_KV_HEADS, Q_GROUP)[None, :, :, None, None]
    (p,) = _sink_softmax([s], sink_b)
    o = jnp.einsum('bhgqk,bkhd->bqhgd', p.astype(v.dtype), v)
    return o.reshape(b, lc, hq * hd)

def _odd_proj(h, w_in):
    cb, cc, cx, cg, q, k, v, ag = _split(
        h @ w_in, [C_WIDTH, C_WIDTH, C_WIDTH, C_WIDTH, ATT_WIDTH, KV_WIDTH, KV_WIDTH, ATT_WIDTH])
    b, l, _ = h.shape
    return (cb, cc, cx, cg,
            q.reshape(b, l, N_Q_HEADS, HEAD_DIM),
            k.reshape(b, l, N_KV_HEADS, HEAD_DIM),
            v.reshape(b, l, N_KV_HEADS, HEAD_DIM), ag)

def _odd_out(cb, cc, cx, cg, att, ag, c_conv_w, w_out):
    y_c = cb * _dwconv(cc * cx, c_conv_w) * jax.nn.silu(cg)
    y_d = att * jax.nn.silu(ag)
    return jnp.concatenate([y_c, y_d], axis=-1) @ w_out

def second_inputs(seed: int = 0) -> dict:
    key = jax.random.key(seed)
    ks = jax.random.split(key, 24)
    ne, no = (DEPTH_2 + 1) // 2, DEPTH_2 // 2

    def nrm(k, shape):
        return jax.random.normal(k, shape, jnp.float32)

    return {
        'x': nrm(ks[0], (BATCH, SEQ, D_MODEL)),
        'c': nrm(ks[1], (BATCH, D_MODEL)),
        'ctx': nrm(ks[2], (BATCH, CTX_LEN, D_MODEL)),
        'c_ctx': nrm(ks[3], (D_MODEL,)),
        'e_norm': 1.0 + 0.02 * nrm(ks[4], (ne, D_MODEL)),
        'e_w_mod': nrm(ks[5], (ne, D_MODEL, 3 * D_MODEL)) * (0.5 * D_MODEL ** -0.5),
        'e_b_mod': 0.02 * nrm(ks[6], (ne, 3 * D_MODEL)),
        'e_w_in': nrm(ks[7], (ne, D_MODEL, EVEN_IN)) * D_MODEL ** -0.5,
        'e_a_conv_w': nrm(ks[8], (ne, A_CONV_W, A_WIDTH)) * A_CONV_W ** -0.5,
        'e_a_conv_b': 0.02 * nrm(ks[9], (ne, A_WIDTH)),
        'e_a_ln_g': 1.0 + 0.02 * nrm(ks[10], (ne, A_WIDTH)),
        'e_a_ln_b': 0.02 * nrm(ks[11], (ne, A_WIDTH)),
        'e_a_pw_w': nrm(ks[12], (ne, A_WIDTH, A_WIDTH)) * A_WIDTH ** -0.5,
        'e_a_pw_b': 0.02 * nrm(ks[13], (ne, A_WIDTH)),
        'e_b_fw': nrm(ks[14], (ne, B_GROUPS, B_GROUP_DIM, B_GROUP_DIM)) * B_GROUP_DIM ** -0.5,
        'e_w_out': nrm(ks[15], (ne, EVEN_MIX, D_MODEL)) * EVEN_MIX ** -0.5,
        'o_norm': 1.0 + 0.02 * nrm(ks[16], (no, D_MODEL)),
        'o_w_mod': nrm(ks[17], (no, D_MODEL, 3 * D_MODEL)) * (0.5 * D_MODEL ** -0.5),
        'o_b_mod': 0.02 * nrm(ks[18], (no, 3 * D_MODEL)),
        'o_w_in': nrm(ks[19], (no, D_MODEL, ODD_IN)) * D_MODEL ** -0.5,
        'o_c_conv_w': nrm(ks[20], (no, C_CONV_W, C_WIDTH)) * C_CONV_W ** -0.5,
        'o_sink': 0.5 * nrm(ks[21], (no, N_Q_HEADS)),
        'o_w_out': nrm(ks[22], (no, ODD_MIX, D_MODEL)) * ODD_MIX ** -0.5,
        'final_norm': 1.0 + 0.02 * nrm(ks[23], (D_MODEL,)),
    }

def second_block(x, c, ctx, c_ctx, e_norm, e_w_mod, e_b_mod, e_w_in, e_a_conv_w, e_a_conv_b,
              e_a_ln_g, e_a_ln_b, e_a_pw_w, e_a_pw_b, e_b_fw, e_w_out,
              o_norm, o_w_mod, o_b_mod, o_w_in, o_c_conv_w, o_sink, o_w_out, final_norm):
    l = x.shape[1]
    rows = l // GRID_W
    row = jnp.broadcast_to(jnp.arange(rows)[:, None], (rows, GRID_W)).reshape(l)
    col = jnp.broadcast_to(jnp.arange(GRID_W)[None, :], (rows, GRID_W)).reshape(l)
    cos, sin = _rope_tables(row, col)
    c_ctx2 = c_ctx[None, :]
    xc = ctx
    for layer in range(DEPTH_2):
        i = layer // 2
        ctx_needed = layer < DEPTH_2 - 1
        if layer % 2 == 0:
            args = (e_w_in[i], e_a_conv_w[i], e_a_conv_b[i], e_a_ln_g[i], e_a_ln_b[i],
                    e_a_pw_w[i], e_a_pw_b[i], e_b_fw[i], e_w_out[i])
            sh, sc, gt = _modulation(c, e_w_mod[i], e_b_mod[i])
            x_new = x + gt * _even_mix(_pre(x, e_norm[i], sh, sc), *args)
            if ctx_needed:
                sh_c, sc_c, gt_c = _modulation(c_ctx2, e_w_mod[i], e_b_mod[i])
                xc = xc + gt_c * _even_mix(_pre(xc, e_norm[i], sh_c, sc_c), *args)
            x = x_new
        else:
            sh, sc, gt = _modulation(c, o_w_mod[i], o_b_mod[i])
            sh_c, sc_c, gt_c = _modulation(c_ctx2, o_w_mod[i], o_b_mod[i])
            cb_c, cc_c, cx_c, cg_c, q_c, k_c, v_c, ag_c = _odd_proj(_pre(xc, o_norm[i], sh_c, sc_c), o_w_in[i])
            cb, cc, cx, cg, q, k, v, ag = _odd_proj(_pre(x, o_norm[i], sh, sc), o_w_in[i])
            att = _window_attention(_apply_rope(q, cos, sin), _apply_rope(k, cos, sin), v, k_c, v_c, o_sink[i])
            x_new = x + gt * _odd_out(cb, cc, cx, cg, att, ag, o_c_conv_w[i], o_w_out[i])
            if ctx_needed:
                att_c = _context_attention(q_c, k_c, v_c, o_sink[i])
                xc = xc + gt_c * _odd_out(cb_c, cc_c, cx_c, cg_c, att_c, ag_c, o_c_conv_w[i], o_w_out[i])
            x = x_new
    return _rmsnorm(x, final_norm)


def setup_inputs(seed=0):
    out = dict(first_inputs(seed))
    for name, value in second_inputs(seed + 1).items():
        if name != "x":
            out[name + "_2"] = value
    return out


def reference(
    x, attn_norm, mlp_norm, final_norm, swa_w_qkv, swa_sinks, swa_w_o, sb_w_qkv, sb_w_o,
    ret_w_in, ret_w_o, mlp_w_up, mlp_w_down, c_2, ctx_2, c_ctx_2, e_norm_2, e_w_mod_2,
    e_b_mod_2, e_w_in_2, e_a_conv_w_2, e_a_conv_b_2, e_a_ln_g_2, e_a_ln_b_2, e_a_pw_w_2,
    e_a_pw_b_2, e_b_fw_2, e_w_out_2, o_norm_2, o_w_mod_2, o_b_mod_2, o_w_in_2, o_c_conv_w_2,
    o_sink_2, o_w_out_2, final_norm_2,
):
    x = first_block(
        x, attn_norm, mlp_norm, final_norm, swa_w_qkv, swa_sinks, swa_w_o, sb_w_qkv, sb_w_o,
        ret_w_in, ret_w_o, mlp_w_up, mlp_w_down,
    )
    return second_block(
        x, c_2, ctx_2, c_ctx_2, e_norm_2, e_w_mod_2, e_b_mod_2, e_w_in_2, e_a_conv_w_2,
        e_a_conv_b_2, e_a_ln_g_2, e_a_ln_b_2, e_a_pw_w_2, e_a_pw_b_2, e_b_fw_2, e_w_out_2,
        o_norm_2, o_w_mod_2, o_b_mod_2, o_w_in_2, o_c_conv_w_2, o_sink_2, o_w_out_2,
        final_norm_2,
    )


_drawn_inputs = setup_inputs


def setup_inputs(seed=0):
    import zlib

    import numpy as np

    out = dict(_drawn_inputs(seed))
    spreads = {}
    factors = {'attn_norm': 5.591,
     'mlp_norm': 3.002,
     'final_norm': 2.846,
     'swa_sinks': 10.853,
     'ctx_2': 45.437,
     'c_ctx_2': 2.942,
     'e_norm_2': 8.0,
     'e_b_mod_2': 5.342,
     'e_a_conv_b_2': 8.0,
     'e_a_ln_g_2': 8.0,
     'e_a_ln_b_2': 8.0,
     'e_a_pw_b_2': 8.0,
     'o_norm_2': 7.615,
     'o_b_mod_2': 3.609,
     'o_sink_2': 8.0,
     'final_norm_2': 24.672}
    for name, (base, spread) in spreads.items():
        noise = np.random.default_rng([zlib.crc32(name.encode()), seed]).standard_normal(out[name].shape)
        drawn = base * np.exp(spread * noise) if base else spread * noise
        out[name] = __import__('jax').numpy.asarray(drawn.astype(out[name].dtype))
    for name, factor in factors.items():
        out[name] = (out[name] * factor).astype(out[name].dtype)
    return out
```

```python
from contextlib import ExitStack

import concourse.bass as bass
from concourse import mybir

ALU = mybir.AluOpType
ACT = mybir.ActivationFunctionType
F32 = mybir.dt.float32
F32R = mybir.dt.float32r
BF16 = mybir.dt.bfloat16

P = 128
D = 1024
KC = D // P
SEQ = 1024
CTX = 256
TOK = SEQ + CTX
TN = 512
NB = SEQ // P
HALF = 4
TAPS = 31
PAD = TAPS // 2
CONV_IN = PAD + SEQ + PAD + CTX + PAD
CONV_OUT = SEQ + PAD + CTX
EPS = 1e-6

STAGES = [("qkv", 10), ("wo", 8), ("mlp", 64), ("ein", 20), ("dft", 6), ("fw", 1), ("pw", 2),
          ("eout", 8), ("oin", 26), ("oout", 8)]
W0 = {}
_n = 0
for _name, _count in STAGES:
    W0[_name] = _n
    _n += _count
UNITS = _n

PARAMS = [("attn_norm", 8), ("mlp_norm", 8), ("final_norm", 8), ("e_norm", 8), ("o_norm", 8),
          ("final_norm2", 8), ("b_mod", 48), ("conv_w", HALF * TAPS), ("conv_b", 4), ("ln_g", 4),
          ("ln_b", 4), ("pw_b", 4), ("c_conv_w", 12), ("sinks", 16), ("o_sink", 8)]
PC = {}
_n = 0
for _name, _count in PARAMS:
    PC[_name] = _n
    _n += _count
NPAR = _n

TILES1 = [(0, TN), (TN, TN)]
TILES2 = [(0, TN), (TN, TN), (SEQ, CTX)]

KB = 1024
A_FIX = 1152
A_WST = A_FIX + 8 * KB
A_WHL = A_WST + 8 * KB
A_R = A_WHL + 16 * KB
A_END = 229368


class Slot:

    def __init__(self, k, scores, turn, exps, sums):
        self.k, self.scores, self.turn, self.exps, self.sums = k, scores, turn, exps, sums


def build(nc, t):
    es = ExitStack()

    def sb(name, shape, at, dtype=F32):
        n = 4 if dtype != BF16 else 2
        for s in shape:
            n *= s
        assert at + n <= A_END, (name, at, n)
        return nc.alloc_sbuf_tensor_at(name, [P, *shape], dtype, offset=at)

    def sem(name):
        return es.enter_context(nc.semaphore(name))

    with es:
        banks = es.enter_context(nc.psum_tensor("banks", [P, 8, TN], F32))

        def bank(b, n=TN):
            return banks[:, b, 0:n]

        at = A_FIX
        par = sb("par", [NPAR], at); at += 4 * NPAR + 32 - (4 * NPAR) % 32
        ident = sb("ident", [P], at); at += 512
        ones = sb("ones", [P], at); at += 512
        inv_d = sb("inv_d", [P], at); at += 512
        swap = sb("swap", [P], at); at += 512
        cds = sb("cds", [2 * P], at); at += 1024
        cdsH = sb("cdsH", [2 * P], at, F32R); at += 1024
        cdsL = sb("cdsL", [2 * P], at, F32R); at += 1024
        modv = sb("modv", [48, 2], at); at += 384
        gmod = sb("gmod", [2, 8, 2], at); at += 128
        stat = sb("stat", [5, 3, 8], at); at += 480
        eps = sb("eps", [1], at); at += 32
        sink8 = sb("sink8", [24], at); at += 96
        assert at <= A_WST, at

        wst = sb("wst", [2, KC * P], A_WST)
        wH = sb("wH", [2, KC * P], A_WHL, F32R)
        wL = sb("wL", [2, KC * P], A_WHL + 8 * KB, F32R)

        stage_loaded = [sem("stage_loaded0"), sem("stage_loaded1")]
        weights_hi = sem("weights_hi")
        weights_split = sem("weights_split")
        units_begun = sem("units_begun")
        W_FREE = 2

        def load_unit(sp, base, i, s):
            u, slot = base + 2 * i + s, (base + s) % 2
            sp.wait_ge(weights_split, u + 1)
            sp.dma_start(wst[:, slot, :], t["wstream"][bass.ds(u, 1)].rearrange("a p f -> p (a f)"))\
                .then_inc(stage_loaded[slot], 16)

        def split_unit(pool, base, i, s):
            u, slot = base + 2 * i + s, (base + s) % 2
            pool.wait_ge(stage_loaded[slot], ((base + s) // 2 + 1 + i) * 16)
            pool.wait_ge(units_begun, u + 1)
            pool.tensor_tensor(wH[:, slot, :], wst[:, slot, :], ones[:, 0:1].to_broadcast([P, KC * P]), ALU.mult)\
                .then_inc(weights_hi, 1)
            pool.wait_ge(weights_hi, u + 1)
            pool.tensor_tensor(wL[:, slot, :], wst[:, slot, :], wH[:, slot, :].bitcast(F32), ALU.subtract)\
                .then_inc(weights_split, 1)

        def stream(eng, one, lo, hi):
            if (hi - lo) // 2 > 1:
                with eng.Fori(0, (hi - lo) // 2) as i:
                    one(eng, lo, i, 0)
                    one(eng, lo, i, 1)
            elif hi - lo >= 2:
                one(eng, lo, 0, 0)
                one(eng, lo, 0, 1)
            if (hi - lo) % 2:
                one(eng, hi - 1, 0, 0)

        def loads(sp, first, last):
            lo = W0[first] + 3 if W0[first] else 0
            hi = min(W0[last] + dict(STAGES)[last] + 3, UNITS)
            stream(sp, load_unit, lo, hi)

        def splits(pool, first, last, done=1):
            lo = W0[first] + done
            hi = min(W0[last] + dict(STAGES)[last] + 1, UNITS)
            stream(pool, split_unit, lo, hi)

        def mm3(pe, out, aH, aL, bH, bL, start, stop):
            first = pe.matmul(out, aH, bH, start=start, stop=False)
            pe.matmul(out, aH, bL, start=False, stop=False)
            return first, pe.matmul(out, aL, bH, start=False, stop=stop)

        def linear_unit(pe, base, i, s, j0, K, tiles, rhs, bank_of, done, drained, ready=None, off=0):
            u, slot = base + 2 * i + s, (base + s) % 2
            T = len(tiles)
            pe.wait_ge(weights_split, u + 1 + W_FREE)
            for ti, (c0, n) in enumerate(tiles):
                j = j0 + ti
                pe.wait_ge(drained, j + 1 + off)
                for k in range(K):
                    if ready:
                        ready(pe, ti, k)
                    w = slice(k * P, k * P + P)
                    f, m = mm3(pe, bank(bank_of(s, ti), n), wH[:, slot, w], wL[:, slot, w],
                               rhs(0, k, c0, n), rhs(1, k, c0, n), k == 0, k == K - 1)
                    if ti == 0 and k == 0:
                        f.then_inc(units_begun, 1)
                m.then_inc(done, 1)

        def linear(pe, base, units, tiles, rhs, done, drained, norm=None):
            T = len(tiles)
            pe.sem_inc(drained, 2 * T)
            if norm:
                first_pair(pe, base, tiles, rhs, lambda s, ti: s * T + ti, done, norm)
            with pe.Fori(1 if norm else 0, units // 2) as i:
                for s in range(2):
                    linear_unit(pe, base, i, s, (2 * i + s) * T, KC, tiles, rhs,
                                lambda s, ti: s * T + ti, done, drained)

        NORM_STEPS = ("sq_ready", "sq_used", "rms_ready", "rstd_ready", "v_ready", "v_shifted", "hi_ready", "ready", "ready_pool")
        norm_sems = {v: sem("norm_" + v) for v in NORM_STEPS}
        norm_counts = dict.fromkeys(NORM_STEPS, 0)
        SQ_SLOTS, V_SLOTS = 3, 4

        squares_done, squares_added, squares_count = sem("squares_done"), sem("squares_added"), [0]

        class Squares:

            FREE = 2

            def __init__(self, name, tiles, at):
                stages_before, done_before = len(squares_count) - 1, sum(squares_count)
                self.squared0, self.added0 = done_before, done_before + self.FREE * stages_before
                squares_count.append(len(tiles) * KC)
                self.acc = sb(name + "_acc", [3, TN], at)
                self.sq = sb(name + "_sq", [2, TN], at + 6 * KB)

            def start(self, dve):
                dve.sem_inc(squares_added, self.FREE - 1)
                dve.memset(self.acc[:], 0.0).then_inc(squares_added, 1)

            def act(self, act, j, slot, x, n):
                act.wait_ge(squares_added, j + (self.added0 + self.FREE - 1))
                act.activation(self.sq[:, slot, 0:n], x, ACT.Square).then_inc(squares_done, 1)

            def dve(self, dve, j, slot, ti, n):
                dve.wait_ge(squares_done, j + (self.squared0 + 1))
                dve.wait_ge(squares_added, j + (self.added0 + self.FREE))
                dve.tensor_tensor(self.acc[:, ti, 0:n], self.acc[:, ti, 0:n], self.sq[:, slot, 0:n], ALU.add)\
                    .then_inc(squares_added, 1)

        class Norm:

            def __init__(self, name, x, tiles, gain, shift, outs, tmp, out32=None, sum_banks=(6, 7), x_ready=None,
                         squares=None, scaled=False):
                self.squares, self.scaled = squares, scaled
                self.x, self.x_ready, self.tiles, self.sum_banks = x, x_ready, tiles, sum_banks
                self.gain, self.shift, self.outs, self.out32 = gain, shift, outs, out32
                self.total = len(tiles) * KC
                self.sq = sb(name + "_sq", [SQ_SLOTS, TN], tmp)
                self.rs = sb(name + "_rs", [len(tiles), TN], tmp + 6 * KB)
                self.v = sb(name + "_v", [V_SLOTS, TN], tmp + 12 * KB)
                self.base = dict(norm_counts)
                split = self.total if outs else 0
                for what, k in (("sq_ready", 0 if squares else self.total),
                                ("sq_used", len(tiles) if squares else self.total), ("rms_ready", len(tiles)),
                                ("rstd_ready", len(tiles)), ("v_ready", split), ("hi_ready", split),
                                ("v_shifted", self.total - self.by_dve(self.total) if shift else 0), ("ready", self.by_dve(self.total)),
                                ("ready_pool", self.total - self.by_dve(self.total))):
                    norm_counts[what] += k

            def wait(self, eng, what, k):
                eng.wait_ge(norm_sems[what], self.base[what] + k)

            def pool_low(self, j):
                return bool(self.outs) and j % 2 == 1 or self.scaled and j % 3 == 2

            def by_dve(self, j):
                return j - sum(self.pool_low(i) for i in range(j))

            def wait_ready(self, eng, j):
                self.wait(eng, "ready", self.by_dve(j))
                if j > self.by_dve(j):
                    self.wait(eng, "ready_pool", j - self.by_dve(j))

            def act(self, act):
                for ti, (c0, n) in enumerate(self.tiles if self.squares else ()):
                    self.wait(act, "sq_used", ti + 1)
                    act.activation(self.rs[:, ti, 0:n], bank(self.sum_banks[ti], n), ACT.Sqrt, bias=eps[:, 0:1])\
                        .then_inc(norm_sems["rms_ready"], 1)
                for j in range(0 if self.squares else self.total):
                    ti, c = divmod(j, KC)
                    if self.x_ready:
                        self.x_ready(act, c, ti)
                    if j >= SQ_SLOTS:
                        self.wait(act, "sq_used", j - SQ_SLOTS + 1)
                    act.activation(self.sq[:, j % SQ_SLOTS, 0:self.tiles[ti][1]], self.x(c, ti), ACT.Square)\
                        .then_inc(norm_sems["sq_ready"], 1)
                    if c == KC - 1:
                        n = self.tiles[ti][1]
                        self.wait(act, "sq_used", (ti + 1) * KC)
                        act.activation(self.rs[:, ti, 0:n], bank(self.sum_banks[ti], n), ACT.Sqrt, bias=eps[:, 0:1])\
                            .then_inc(norm_sems["rms_ready"], 1)
                for j in range(self.total if self.outs else 0):
                    ti, c = divmod(j, KC)
                    self.wait(act, "v_ready", j + 1)
                    v, shift = self.v[:, j % V_SLOTS, 0:self.tiles[ti][1]], self.shift(c, ti) if self.shift else 0.0
                    if self.shift and self.pool_low(j):
                        act.activation(v, v, ACT.Identity, bias=shift).then_inc(norm_sems["v_shifted"], 1)
                        self.wait(act, "v_shifted", j - self.by_dve(j) + 1)
                        shift = 0.0
                    act.activation(self.outs(0, c, ti), v, ACT.Identity, bias=shift).then_inc(norm_sems["hi_ready"], 1)

            def pe(self, pe):
                if self.squares:
                    pe.wait_ge(squares_added, self.squares.added0 + self.squares.FREE + self.total)
                    for ti, (c0, n) in enumerate(self.tiles):
                        pe.matmul(bank(self.sum_banks[ti], n), inv_d[:], self.squares.acc[:, ti, 0:n], start=True,
                                  stop=True).then_inc(norm_sems["sq_used"], 1)
                    return
                for j in range(self.total):
                    ti, c = divmod(j, KC)
                    n = self.tiles[ti][1]
                    self.wait(pe, "sq_ready", j + 1)
                    pe.matmul(bank(self.sum_banks[ti], n), inv_d[:], self.sq[:, j % SQ_SLOTS, 0:n], start=c == 0,
                              stop=c == KC - 1).then_inc(norm_sems["sq_used"], 1)

            def pool(self, pool):
                for j in range(self.total):
                    if self.scaled and self.pool_low(j):
                        ti, c = divmod(j, KC)
                        self.wait(pool, "rstd_ready", ti + 1)
                        pool.tensor_tensor(self.out32(c, ti), self.x(c, ti), self.rs[:, ti, 0:self.tiles[ti][1]], ALU.mult)\
                            .then_inc(norm_sems["ready_pool"], 1)
                    elif self.pool_low(j):
                        self.low(pool, j, norm_sems["ready_pool"])

            def low(self, eng, j, signal):
                ti, c = divmod(j, KC)
                v = self.v[:, j % V_SLOTS, 0:self.tiles[ti][1]]
                H, L = self.outs(0, c, ti).bitcast(F32), self.outs(1, c, ti)
                self.wait(eng, "hi_ready", j + 1)
                if self.shift and not self.pool_low(j):
                    eng.scalar_tensor_tensor(L, v, self.shift(c, ti), H, ALU.add, ALU.subtract).then_inc(signal, 1)
                else:
                    eng.tensor_tensor(L, v, H, ALU.subtract).then_inc(signal, 1)

            def dve(self, dve):
                for j in range(self.total):
                    ti, c = divmod(j, KC)
                    n = self.tiles[ti][1]
                    if c == 0:
                        self.wait(dve, "rms_ready", ti + 1)
                        dve.reciprocal(self.rs[:, ti, 0:n], self.rs[:, ti, 0:n]).then_inc(norm_sems["rstd_ready"], 1)
                        self.wait(dve, "rstd_ready", ti + 1)
                    if self.scaled:
                        if not self.pool_low(j):
                            dve.tensor_tensor(self.out32(c, ti), self.x(c, ti), self.rs[:, ti, 0:n], ALU.mult)\
                                .then_inc(norm_sems["ready"], 1)
                        continue
                    if self.outs is None:
                        dve.scalar_tensor_tensor(self.out32(c, ti), self.x(c, ti), self.gain(c, ti),
                                                 self.rs[:, ti, 0:n], ALU.mult, ALU.mult).then_inc(norm_sems["ready"], 1)
                        continue
                    if j >= V_SLOTS:
                        self.wait_ready(dve, j - V_SLOTS + 1)
                    dve.scalar_tensor_tensor(self.v[:, j % V_SLOTS, 0:n], self.x(c, ti), self.gain(c, ti),
                                             self.rs[:, ti, 0:n], ALU.mult, ALU.mult).then_inc(norm_sems["v_ready"], 1)
                    if j >= 1 and not self.pool_low(j - 1):
                        self.low(dve, j - 1, norm_sems["ready"])
                if self.outs and not self.pool_low(self.total - 1):
                    self.low(dve, self.total - 1, norm_sems["ready"])

        def first_pair(pe, base, tiles, rhs, bank_of, done, norm):
            def product(s, ti, k):
                c0, n = tiles[ti]
                w, slot = slice(k * P, k * P + P), (base + s) % 2
                return mm3(pe, bank(bank_of(s, ti), n), wH[:, slot, w], wL[:, slot, w], rhs(0, k, c0, n),
                           rhs(1, k, c0, n), k == 0, k == KC - 1)

            pe.wait_ge(weights_split, base + 1 + W_FREE)
            for k in range(KC):
                norm.wait_ready(pe, k + 1)
                _, m = product(0, 0, k)
                if k == 0:
                    pe.wait_ge(weights_split, base + 2 + W_FREE)
                if k < KC - 1:
                    product(1, 0, k)
            m.then_inc(done, 1)
            for ti in range(1, len(tiles)):
                for k in range(KC):
                    norm.wait_ready(pe, ti * KC + k + 1)
                    _, m = product(0, ti, k)
                m.then_inc(done, 1)
            _, m = product(1, 0, KC - 1)
            m.then_inc(done, 1)
            for ti in range(1, len(tiles)):
                for k in range(KC):
                    f, m = product(1, ti, k)
                    if ti == 1 and k == 0:
                        f.then_inc(units_begun, 1)
                m.then_inc(done, 1)

        def cols(tensor):
            return lambda c, c0, n: tensor[:, c, c0:c0 + n]

        def hl(tH, tL):
            return lambda part, k, c0, n: (tL if part else tH)[:, k, c0:c0 + n]

        def pcol(name, c):
            return par[:, PC[name] + c:PC[name] + c + 1]

        h = sb("h", [KC, SEQ], A_R)
        uH = sb("uH", [KC, SEQ], A_R + 32 * KB, F32R)
        uL = sb("uL", [KC, SEQ], A_R + 64 * KB, F32R)
        aH = sb("aH", [KC, SEQ], A_R + 96 * KB, F32R)
        aL = sb("aL", [KC, SEQ], A_R + 128 * KB, F32R)
        RX = A_R + 160 * KB
        kH = sb("kH", [SEQ], RX, F32R)
        kL = sb("kL", [SEQ], RX + 4 * KB, F32R)
        vT = sb("vT", [SEQ], RX + 8 * KB)
        vz1H = sb("vz1H", [NB, 2, P], RX + 12 * KB, F32R)
        vz1L = sb("vz1L", [NB, 2, P], RX + 20 * KB, F32R)
        bias8 = sb("bias8", [16, 256], A_R)
        bias_loaded = sem("bias_loaded")

        par_loaded, vz1_zero = sem("par_loaded"), sem("vz1_zero")
        x_loaded = [sem(f"x_loaded{i}") for i in range(4)]
        norm1 = Norm("norm1", lambda c, ti: h[:, c, TN * ti:TN * ti + TN], TILES1,
                     lambda c, ti: pcol("attn_norm", c), None,
                     lambda part, c, ti: (uL if part else uH)[:, c, TN * ti:TN * ti + TN], A_R + 140 * KB,
                     x_ready=lambda eng, c, ti: eng.wait_ge(x_loaded[2 * ti + c // 4], 16))
        consts_set, qkv_done, qkv_hi, qkv_drained, cds_hi = (sem("consts_set"), sem("qkv_done"), sem("qkv_hi"),
                                                     sem("qkv_drained"), sem("cds_hi"))
        with nc.Block() as block:
            @block.sync
            def _(sp):
                for part, loaded in enumerate(x_loaded):
                    ti, c = part // 2, part % 2 * 4
                    sp.dma_start(h[:, c:c + 4, TN * ti:TN * ti + TN], t["x"][:, c:c + 4, TN * ti:TN * ti + TN])\
                        .then_inc(loaded, 16)
                sp.dma_start(par[:], t["par"]).then_inc(par_loaded, 16)
                sp.dma_start(ident[:], t["ident"]).then_inc(par_loaded, 16)
                sp.dma_start(swap[:], t["swap"]).then_inc(par_loaded, 16)
                sp.dma_start(cds[:], t["cds"]).then_inc(par_loaded, 16)
                loads(sp, "qkv", "qkv")

            @block.gpsimd
            def _(pool):
                pool.sem_inc(weights_split, W_FREE)
                pool.memset(ones[:], 1.0).then_inc(consts_set, 1)
                pool.memset(inv_d[:], 1.0 / D).then_inc(consts_set, 1)
                pool.memset(eps[:], EPS).then_inc(consts_set, 1)
                pool.wait_ge(consts_set, 3)
                pool.memset(vz1H[:].bitcast(F32), 0.0).then_inc(vz1_zero, 1)
                pool.memset(vz1L[:].bitcast(F32), 0.0).then_inc(vz1_zero, 1)
                split_unit(pool, W0["qkv"], 0, 0)
                split_unit(pool, W0["qkv"] + 1, 0, 0)
                norm1.pool(pool)
                splits(pool, "qkv", "qkv", 2)

            @block.scalar
            def _(act):
                act.wait_ge(consts_set, 3)
                norm1.act(act)
                norm1.wait_ready(act, 2 * KC)
                act.dma_start(bias8[:], t["bias8"]).then_inc(bias_loaded, 16)
                act.wait_ge(par_loaded, 64)
                act.copy(cdsH[:], cds[:]).then_inc(cds_hi, 1)
                def hi(i, s, dst):
                    for ti in range(2):
                        j = (2 * i + s) * 2 + ti
                        act.wait_ge(qkv_done, j + 1)
                        act.copy(dst(ti), bank(s * 2 + ti)).then_inc(qkv_hi, 1)
                with act.Fori(0, 4) as i:
                    for s in range(2):
                        hi(i, s, lambda ti: aH[:, bass.ds(2 * i + s, 1), TN * ti:TN * ti + TN].rearrange("p a n -> p (a n)"))
                hi(4, 0, lambda ti: kH[:, TN * ti:TN * ti + TN])
                hi(4, 1, lambda ti: vT[:, TN * ti:TN * ti + TN])

            @block.vector
            def _(dve):
                dve.wait_ge(par_loaded, 64)
                dve.wait_ge(consts_set, 3)
                norm1.dve(dve)
                dve.wait_ge(cds_hi, 1)
                dve.tensor_tensor(cdsL[:], cds[:], cdsH[:].bitcast(F32), ALU.subtract)
                dve.tensor_scalar(sink8[:], par[:, PC["sinks"]:PC["sinks"] + 24], 8.0, None, ALU.mult)

                def lo(i, s, H, L):
                    for ti in range(2):
                        j = (2 * i + s) * 2 + ti
                        dve.wait_ge(qkv_hi, j + 1)
                        dve.tensor_tensor(L(ti), bank(s * 2 + ti), H(ti).bitcast(F32), ALU.subtract)\
                            .then_inc(qkv_drained, 1)
                with dve.Fori(0, 4) as i:
                    for s in range(2):
                        lo(i, s, *[(lambda ti, a=a: a[:, bass.ds(2 * i + s, 1), TN * ti:TN * ti + TN]
                                    .rearrange("p a n -> p (a n)")) for a in (aH, aL)])
                lo(4, 0, lambda ti: kH[:, TN * ti:TN * ti + TN], lambda ti: kL[:, TN * ti:TN * ti + TN])

            @block.tensor
            def _(pe):
                pe.sem_inc(units_begun, 2)
                pe.wait_ge(consts_set, 3)
                norm1.pe(pe)
                linear(pe, W0["qkv"], 10, TILES1, hl(uH, uL), qkv_done, qkv_drained, norm1)

        def attention(name, steps, s_tiles, t_tiles, heads, W, QH, QL, KH, KL, vzH, vzL, in1, sink_of,
                      Lat, PTat, nslots, gate=None, vsrc=None, vblocks=0, chain_max=False, waits=(), zeroed=None):
            S_RING, T_RING, T_BANK, O_BANK = 3, 3, 3, 6
            logits = sb(name + "_logits", [3, heads, W], Lat)
            pTH = sb(name + "_pTH", [nslots, TN], PTat, F32R)
            pTL = sb(name + "_pTL", [nslots, TN], PTat + nslots * 2 * KB, F32R)
            (s_done, s_free, t_done, p_hi, p_lo, pv_done, o_hi, o_lo, neg_ready, exp_done,
             den_ready, rden_ready, normed0, normed1, v_done, v_hi, v_lo, step1) = (
                sem(f"{name}_{x}") for x in (
                    "s_done s_free t_done p_hi p_lo pv_done o_hi o_lo neg_ready exp_done "
                    "den_ready rden_ready normed0 normed1 v_done v_hi v_lo step1").split())
            vz_zero = zeroed or sem(name + "_vz_zero")
            gated = sem(name + "_gated") if gate else None
            N = len(steps)
            sidx, tidx = [0], [0]
            for st in steps:
                sidx.append(sidx[-1] + len(s_tiles(st)))
                tidx.append(tidx[-1] + len(t_tiles(st)))
            plan = []
            for k in range(N + 2):
                ns = len(s_tiles(steps[k])) if k < N else 0
                nt = len(t_tiles(steps[k - 2])) if k >= 2 else 0
                ne = heads if 1 <= k <= N else 0
                a_slot = 1 if ns <= nt else 2
                per = heads if nt <= 2 else 3 if nt == 4 else 2
                exps = (ne + per - 1) // per
                extra = 1 if nt else 0
                for x in range(max((ns + a_slot - 1) // a_slot, nt, exps + 1)):
                    plan.append(Slot(k, [y for y in range(a_slot * x + (extra if x else 0), a_slot * (x + 1) + extra) if y < ns],
                                     (k - 2, x) if x < nt else None, range(per * x, min(per * x + per, ne)),
                                     ne and x == exps))
            plan += [Slot(N + 2, [], None, range(0), False)] * 3

            values_at = [slot.k for slot in plan].index(1)

            def turned(i, ago):
                return plan[i - ago].turn if i >= ago else None

            def finished(i):
                tile = turned(i, 3)
                return tile[0] if tile and tile[1] == len(t_tiles(steps[tile[0]])) - 1 else None

            MX, MX2, NEG, ES, SUM = range(5)
            mx = MX2 if chain_max else MX

            def ranges(st):
                offs = [(e[5], e[5] + e[4]) for x in s_tiles(st) for e in x]
                return min(a for a, b in offs), max(b for a, b in offs)

            def out_low(eng, k):
                n, cg = steps[k]
                eng.wait_ge(o_hi, k + 1)
                dst = [a[:, 4 * cg:4 * cg + 4, n * P:n * P + P] for a in (QH, QL)]
                src = gate["tmp"] if gate else banks[:, O_BANK + k % 2, :].rearrange("p (c q) -> p c q", c=4)
                eng.tensor_tensor(dst[1], src, dst[0].bitcast(F32), ALU.subtract).then_inc(o_lo, 1)

            with nc.Block() as block:
                @block.sync
                def _(sp):
                    if gate:
                        sp.wait_ge(*gate["stored"])
                        for k in range(N):
                            if k >= 2:
                                sp.wait_ge(gated, k - 1)
                            sp.dma_start(gate["tile"](k % 2), gate["source"](steps[k][0])).then_inc(gate["loaded"][k % 2], 16)

                @block.tensor
                def _(pe):
                    def values():
                        for b in range(vblocks):
                            m = pe.transpose(banks[:, T_BANK + b // 4, (b % 4) * P:(b % 4 + 1) * P],
                                             vsrc[:, b * P:(b + 1) * P], ident[:])
                            if b % 4 == 3 or b == vblocks - 1:
                                m.then_inc(v_done, 1)

                    for sm, val in waits:
                        pe.wait_ge(sm, val)

                    def score(k, x):
                        g = sidx[k] + x
                        if g >= S_RING:
                            pe.wait_ge(s_free, g - S_RING + 1)
                        n, cg = steps[k]
                        for y, (hs, kv, c, col, w, off, boff) in enumerate(s_tiles(steps[k])[x]):
                            rows = slice(64 * kv, 64 * kv + 64)
                            q = slice(n * P, n * P + P)
                            _, m = mm3(pe, banks[:, g % S_RING, boff:boff + w], QH[rows, c, q], QL[rows, c, q],
                                       KH[rows, col:col + w], KL[rows, col:col + w], True, True)
                        m.then_inc(s_done, 1)

                    def turn(k, x):
                        g = tidx[k] + x
                        kv, vb, off = t_tiles(steps[k])[x]
                        if g >= T_RING:
                            pe.wait_ge(p_lo, g - T_RING + 1)
                        if g == 0:
                            pe.wait_ge(v_lo, (vblocks + 3) // 4)
                        if x == 0:
                            pe.wait_ge(normed0, k + 1)
                        if 2 * x == len(t_tiles(steps[k])):
                            pe.wait_ge(normed1, k + 1)
                        for ci in range(4):
                            m = pe.transpose(banks[:, T_BANK + g % T_RING, ci * P:ci * P + P],
                                             logits[:, k % 3, 2 * ci + kv, off:off + P], ident[:])
                        m.then_inc(t_done, 1)

                    def weigh(k, x):
                        g = tidx[k] + x
                        kv, vb, off = t_tiles(steps[k])[x]
                        last = x == len(t_tiles(steps[k])) - 1
                        if x == 0 and k >= 2:
                            pe.wait_ge(o_lo, k - 1)
                        pe.wait_ge(p_lo, g + 1)
                        _, m = mm3(pe, bank(O_BANK + k % 2), vzH[:, vb, kv, :], vzL[:, vb, kv, :], pTH[:, g % nslots, :],
                                   pTL[:, g % nslots, :], x == 0, last)
                        m.then_inc(pv_done, 1)

                    for i, slot in enumerate(plan):
                        for y in slot.scores:
                            score(slot.k, y)
                        if i == values_at:
                            values()
                        if slot.turn:
                            turn(*slot.turn)
                        if turned(i, 2):
                            weigh(*turned(i, 2))

                @block.vector
                def _(dve):
                    if not zeroed:
                        dve.memset(vzL[:].bitcast(F32), 0.0).then_inc(vz_zero, 1)

                    def values_low():
                        for b in range((vblocks + 3) // 4):
                            n = min(4, vblocks - 4 * b)
                            dve.wait_ge(v_hi, 2 * b + 2)
                            for kv in range(2):
                                f = slice(64 * kv, 64 * kv + 64)
                                m = dve.tensor_tensor(vzL[:, 4 * b:4 * b + n, kv, f],
                                                      banks[:, T_BANK + b, 0:n * P].rearrange("p (b f) -> p b f", b=n)[:, :, f],
                                                      vzH[:, 4 * b:4 * b + n, kv, f].bitcast(F32), ALU.subtract)
                            m.then_inc(v_lo, 1)

                    def logit(k, x):
                        g = sidx[k] + x
                        dve.wait_ge(s_done, g + 1)
                        tiles = s_tiles(steps[k])[x]
                        if tiles[0][5] >= 384:
                            dve.wait_ge(s_free, g)
                        for y, (hs, kv, c, col, w, off, boff) in enumerate(tiles):
                            head = kv * (heads_all // 2) + c
                            if off >= 384:
                                init, acc = stat[:, MX, k % 3, hs:hs + 1], stat[:, MX2, k % 3, hs:hs + 1]
                            else:
                                init = sink8[:, sink_of(head):sink_of(head) + 1]
                                acc = stat[:, MX, k % 3, hs:hs + 1]
                            m = dve.tensor_tensor_reduce(
                                out=logits[:, k % 3, hs, off:off + w], in0=banks[:, g % S_RING, boff:boff + w],
                                in1=in1(head, off, w, steps[k]), scale=1.0, scalar=init, op0=ALU.add, op1=ALU.max,
                                accum_out=acc)
                        m.then_inc(s_free, 1)

                    heads_all = 16 if not chain_max else 8

                    def low(k, x):
                        g = tidx[k] + x
                        dve.wait_ge(p_hi, g + 1)
                        dve.tensor_tensor(pTL[:, g % nslots, :], bank(T_BANK + g % T_RING), pTH[:, g % nslots, :].bitcast(F32),
                                          ALU.subtract).then_inc(p_lo, 1)

                    def neg_max(k):
                        n, cg = steps[k]
                        s0 = PC["o_sink"] if chain_max else PC["sinks"]
                        dve.wait_ge(s_free, sidx[k + 1])
                        dve.tensor_scalar(stat[:, NEG, k % 3, :], stat[:, mx, k % 3, :], -0.125, None, ALU.mult)\
                            .then_inc(step1, 1)
                        dve.wait_ge(step1, k + 1)
                        sk = par[:, s0:s0 + heads_all].rearrange("p (v c) -> p c v", v=2)[:, 4 * cg:4 * cg + 4, :]
                        dve.tensor_tensor(stat[:, ES, k % 3, :].rearrange("p (c v) -> p c v", v=2),
                                          stat[:, NEG, k % 3, :].rearrange("p (c v) -> p c v", v=2), sk, ALU.add)\
                            .then_inc(neg_ready, 1)

                    def denominators(k):
                        dve.wait_ge(exp_done, k + 1)
                        dve.tensor_tensor(stat[:, SUM, k % 3, :], stat[:, SUM, k % 3, :], stat[:, ES, k % 3, :], ALU.add)\
                            .then_inc(den_ready, 1)
                        dve.wait_ge(den_ready, k + 1)
                        dve.reciprocal(stat[:, SUM, k % 3, :], stat[:, SUM, k % 3, :]).then_inc(rden_ready, 1)
                        dve.wait_ge(rden_ready, k + 1)
                        lo, hi = ranges(steps[k])
                        for hs in range(0, heads, 2):
                            src = logits[:, k % 3, hs, lo:hi]
                            m = dve.tensor_scalar(src, src, stat[:, SUM, k % 3, hs:hs + 1], None, ALU.mult)
                        m.then_inc(normed0, 1)

                    def gate_out(k):
                        dve.wait_ge(pv_done, tidx[k + 1])
                        dve.wait_ge(gate["loaded"][k % 2], 16 * (k // 2 + 1))
                        if k >= 1:
                            dve.wait_ge(o_lo, k)
                        dve.tensor_tensor(gate["tmp"], banks[:, O_BANK + k % 2, :].rearrange("p (c q) -> p c q", c=4),
                                          gate["tile"](k % 2), ALU.mult).then_inc(gated, 1)

                    for i, slot in enumerate(plan):
                        done = finished(i)
                        if done is not None and gate:
                            gate_out(done)
                        if slot.sums:
                            denominators(slot.k - 1)
                        if turned(i, 1):
                            low(*turned(i, 1))
                        for y in slot.scores:
                            logit(slot.k, y)
                            if y == len(s_tiles(steps[slot.k])) - 1:
                                neg_max(slot.k)
                        if done is not None and not gate:
                            out_low(dve, done)
                        if i == values_at:
                            values_low()

                @block.scalar
                def _(act):
                    def values_high():
                        for b in range((vblocks + 3) // 4):
                            n = min(4, vblocks - 4 * b)
                            act.wait_ge(v_done, b + 1)
                            act.wait_ge(vz_zero, 2)
                            for kv in range(2):
                                f = slice(64 * kv, 64 * kv + 64)
                                act.copy(vzH[:, 4 * b:4 * b + n, kv, f],
                                         banks[:, T_BANK + b, 0:n * P].rearrange("p (b f) -> p b f", b=n)[:, :, f]).then_inc(v_hi, 1)

                    def tile_high(k, x):
                        g = tidx[k] + x
                        act.wait_ge(t_done, g + 1)
                        if g >= nslots:
                            act.wait_ge(pv_done, g - nslots + 1)
                        act.copy(pTH[:, g % nslots, :], bank(T_BANK + g % T_RING)).then_inc(p_hi, 1)

                    def out_high(k):
                        n, cg = steps[k]
                        if gate:
                            act.wait_ge(gated, k + 1)
                        else:
                            act.wait_ge(pv_done, tidx[k + 1])
                        src = gate["tmp"] if gate else banks[:, O_BANK + k % 2, :].rearrange("p (c q) -> p c q", c=4)
                        act.copy(QH[:, 4 * cg:4 * cg + 4, n * P:n * P + P], src).then_inc(o_hi, 1)

                    def exponentials(k, which):
                        if which[0] == 0:
                            act.wait_ge(neg_ready, k + 1)
                            act.activation(stat[:, ES, k % 3, :], stat[:, ES, k % 3, :], ACT.Exp)
                        lo, hi = ranges(steps[k])
                        for hs in which:
                            src = logits[:, k % 3, hs, lo:hi]
                            m = act.activation(src, src, ACT.Exp, bias=stat[:, NEG, k % 3, hs:hs + 1], scale=0.125,
                                               accum_out=stat[:, SUM, k % 3, hs:hs + 1])
                        if which[-1] == heads - 1:
                            m.then_inc(exp_done, 1)

                    for i, slot in enumerate(plan):
                        if i == values_at:
                            values_high()
                        if slot.exps and heads * W > 4096:
                            exponentials(slot.k - 1, slot.exps)
                        if slot.turn:
                            tile_high(*slot.turn)
                        if finished(i) is not None:
                            out_high(finished(i))
                        if slot.exps and heads * W <= 4096:
                            exponentials(slot.k - 1, slot.exps)

                @block.gpsimd
                def _(pool):
                    if not zeroed:
                        pool.memset(vzH[:].bitcast(F32), 0.0).then_inc(vz_zero, 1)
                    def divide(k):
                        pool.wait_ge(rden_ready, k + 1)
                        lo, hi = ranges(steps[k])
                        for hs in range(1, heads, 2):
                            src = logits[:, k % 3, hs, lo:hi]
                            m = pool.tensor_scalar(src, src, stat[:, SUM, k % 3, hs:hs + 1], None, ALU.mult)
                        m.then_inc(normed1, 1)

                    for i, slot in enumerate(plan):
                        if slot.sums:
                            divide(slot.k - 1)
                        if gate and finished(i) is not None:
                            out_low(pool, finished(i))



        def s_tiles1(st):
            n, cg = st
            lo = P if n == 0 else 0
            return [[(2 * ci + kv, kv, 4 * cg + ci, (n - 1) * P + lo, 256 - lo, lo, 256 * (ci % 2) + lo)
                     for ci in (c2, c2 + 1)] for c2 in (0, 2) for kv in range(2)]

        def t_tiles1(st):
            n, cg = st
            return [(kv, n - 1 + sblk, sblk * P) for kv in range(2) for sblk in range(1 if n == 0 else 0, 2)]

        attention("swa", [(n, cg) for n in range(NB) for cg in range(2)], s_tiles1, t_tiles1, 8, 256, aH, aL, kH, kL,
                  vz1H, vz1L, lambda head, off, w, st: bias8[:, head, off:off + w], lambda head: head,
                  A_R + 48 * KB, A_R + 16 * KB, 5, vsrc=vT, vblocks=NB, zeroed=vz1_zero,
                  waits=[(bias_loaded, 16)])

        x_again, wo_done, wo_drained = sem("x_again"), sem("wo_done"), sem("wo_drained")
        wo_squares = Squares("wo_squares", TILES1, A_R + 32 * KB)
        with nc.Block() as block:
            @block.sync
            def _(sp):
                sp.dma_start(h[:], t["x"]).then_inc(x_again, 16)
                loads(sp, "wo", "wo")

            @block.scalar
            def _(act):
                with act.Fori(0, 4) as i:
                    for s in range(2):
                        for ti in range(2):
                            j = (2 * i + s) * 2 + ti
                            act.wait_ge(wo_drained, j + 1 + 4)
                            wo_squares.act(act, j, ti, h[:, bass.ds(2 * i + s, 1), TN * ti:TN * ti + TN]
                                           .rearrange("p a n -> p (a n)"), TN)

            @block.gpsimd
            def _(pool):
                splits(pool, "wo", "wo")

            @block.vector
            def _(dve):
                wo_squares.start(dve)
                dve.wait_ge(x_again, 16)
                with dve.Fori(0, 4) as i:
                    for s in range(2):
                        for ti in range(2):
                            dve.wait_ge(wo_done, (2 * i + s) * 2 + ti + 1)
                            dst = h[:, bass.ds(2 * i + s, 1), TN * ti:TN * ti + TN].rearrange("p a n -> p (a n)")
                            dve.tensor_tensor(dst, bank(s * 2 + ti), dst, ALU.add).then_inc(wo_drained, 1)
                            wo_squares.dve(dve, (2 * i + s) * 2 + ti, ti, ti, TN)

            @block.tensor
            def _(pe):
                linear(pe, W0["wo"], 8, TILES1, hl(aH, aL), wo_done, wo_drained)

        QUARTERS, R_SLOTS, MODS = 4, 2, 3
        norm2 = Norm("norm2", lambda c, ti: h[:, c, TN * ti:TN * ti + TN], TILES1,
                     lambda c, ti: pcol("mlp_norm", c), None,
                     lambda part, c, ti: (uL if part else uH)[:, c, TN * ti:TN * ti + TN], A_R + 140 * KB, squares=wo_squares)
        cvec = sb("cvec", [2, D], RX)
        mod_w = sb("mod_w", [MODS, D], RX + 8 * KB)
        mod_junk = sb("mod_junk", [D], RX + 20 * KB, BF16)
        relu = sb("relu", [R_SLOTS, TN], RX + 22 * KB)
        asq = sb("asq", [R_SLOTS, TN], RX + 26 * KB)
        (cvec_loaded, cvec_silu, up_done, up_drained, a_hi, a_sq, a_lo, down_done, down_drained, mod_sum) = (
            sem(x) for x in ("cvec_loaded cvec_silu up_done up_drained a_hi a_sq a_lo down_done down_drained "
                             "mod_sum").split())
        mlp_squares = Squares("mlp_squares", TILES1, A_R + 48 * KB)
        mod_loaded = [sem(f"mod_loaded{i}") for i in range(MODS)]
        base = W0["mlp"]
        with nc.Block() as block:
            @block.sync
            def _(sp):
                sp.dma_start(cvec[:], t["cvec"]).then_inc(cvec_loaded, 16)
                with sp.Fori(0, QUARTERS) as q:
                    with sp.Fori(0, 4) as i:
                        for s in range(2):
                            load_unit(sp, base + 3, i + q * 8, s)
                        for m in range(MODS):
                            n = 12 * q + 3 * i + m
                            sp.wait_ge(mod_sum, 2 * n + 1)
                            sp.dma_start(mod_w[:, m, :], t["mod_w"][bass.ds(n, 1)].rearrange("a p f -> p (a f)"))\
                                .then_inc(mod_loaded[m], 16)
                    with sp.Fori(0, 4) as i:
                        for s in range(2):
                            load_unit(sp, base + 3, i + q * 8 + 4, s)

            @block.gpsimd
            def _(pool):
                split_unit(pool, base + 1, 0, 0)
                norm2.pool(pool)
                splits(pool, "mlp", "mlp", 2)

            @block.scalar
            def _(act):
                norm2.act(act)
                act.wait_ge(cvec_loaded, 16)
                act.activation(cvec[:], cvec[:], ACT.Silu).then_inc(cvec_silu, 1)
                def hidden(q):
                    with act.Fori(0, 4) as i:
                        for s in range(2):
                            for ti in range(2):
                                j = q * 16 + (2 * i + s) * 2 + ti
                                act.wait_ge(up_done, j + 1)
                                act.wait_ge(a_lo, j + 1)
                                act.activation(relu[:, ti, :], bank(s * 2 + ti), ACT.Relu).then_inc(up_drained, 1)
                                act.wait_ge(up_drained, j + 1 + 4)
                                act.activation(aH[:, bass.ds(2 * i + s, 1), TN * ti:TN * ti + TN]
                                               .rearrange("p a n -> p (a n)"), relu[:, ti, :], ACT.Square).then_inc(a_hi, 1)

                with act.Fori(0, QUARTERS - 1) as q:
                    hidden(q)
                hidden(QUARTERS - 1)
                with act.Fori(0, 4) as i:
                    for s in range(2):
                        for ti in range(2):
                            j = (2 * i + s) * 2 + ti
                            act.wait_ge(down_drained, (QUARTERS - 1) * 16 + j + 1 + 4)
                            mlp_squares.act(act, j, ti, h[:, bass.ds(2 * i + s, 1), TN * ti:TN * ti + TN]
                                            .rearrange("p a n -> p (a n)"), TN)

            @block.vector
            def _(dve):
                dve.sem_inc(a_lo, R_SLOTS)
                dve.sem_inc(mod_sum, 2 * MODS - 1)
                norm2.dve(dve)
                dve.wait_ge(cvec_silu, 1)
                def hidden(q):
                    with dve.Fori(0, 4) as i:
                        for s in range(2):
                            for ti in range(2):
                                j = q * 16 + (2 * i + s) * 2 + ti
                                dve.wait_ge(up_drained, j + 1 + 4)
                                dve.tensor_tensor(asq[:, ti, :], relu[:, ti, :], relu[:, ti, :], ALU.mult).then_inc(a_sq, 1)
                                dve.wait_ge(a_sq, j + 1)
                                dve.wait_ge(a_hi, j + 1)
                                H, L = (a[:, bass.ds(2 * i + s, 1), TN * ti:TN * ti + TN].rearrange("p a n -> p (a n)")
                                        for a in (aH, aL))
                                dve.tensor_tensor(L, asq[:, ti, :], H.bitcast(F32), ALU.subtract).then_inc(a_lo, 1)
                        for m in range(MODS):
                            dve.wait_ge(mod_loaded[m], (q * 4 + i + 1) * 16)
                            n = 12 * q + 3 * i + m
                            for v in range(2):
                                dve.wait_ge(mod_sum, 2 * n + v + 5)
                                dve.scalar_tensor_tensor(
                                    mod_junk[:], mod_w[:, m, :], 1.0, cvec[:, v, :], ALU.mult, ALU.mult,
                                    accum_out=modv[:, bass.ds(12 * q + 3 * i + m, 1), v:v + 1].rearrange("p a n -> p (a n)"))\
                                    .then_inc(mod_sum, 1)

                def down(q, squares=None):
                    with dve.Fori(0, 4) as i:
                        for s in range(2):
                            for ti in range(2):
                                j = q * 16 + (2 * i + s) * 2 + ti
                                dve.wait_ge(down_done, j + 1)
                                dst = h[:, bass.ds(2 * i + s, 1), TN * ti:TN * ti + TN].rearrange("p a n -> p (a n)")
                                dve.tensor_tensor(dst, bank(4 + s * 2 + ti), dst, ALU.add).then_inc(down_drained, 1)
                                if squares:
                                    squares.dve(dve, (2 * i + s) * 2 + ti, ti, ti, TN)

                with dve.Fori(0, QUARTERS - 1) as q:
                    hidden(q)
                    down(q)
                hidden(QUARTERS - 1)
                mlp_squares.start(dve)
                down(QUARTERS - 1, mlp_squares)

            @block.tensor
            def _(pe):
                pe.sem_inc(units_begun, 1)
                norm2.pe(pe)
                pe.sem_inc(up_drained, 4)
                pe.sem_inc(down_drained, 4)

                def up(q, first):
                    with pe.Fori(first, 4) as i:
                        for s in range(2):
                            linear_unit(pe, base, i + q * 8, s, q * 16 + (2 * i + s) * 2, KC, TILES1, hl(uH, uL),
                                        lambda s, ti: s * 2 + ti, up_done, up_drained)

                def down(q):
                    with pe.Fori(0, 4) as i:
                        for s in range(2):
                            linear_unit(pe, base, i + q * 8 + 4, s, q * 16 + (2 * i + s) * 2, KC, TILES1, hl(aH, aL),
                                        lambda s, ti: 4 + s * 2 + ti, down_done, down_drained,
                                        lambda pe, ti, k: pe.wait_ge(a_lo, q * 16 + (2 * k + ti + 1 + R_SLOTS)))

                first_pair(pe, base, TILES1, hl(uH, uL), lambda s, ti: s * 2 + ti, up_done, norm2)
                up(0, 1)
                norm2.wait(pe, "rstd_ready", 2)
                down(0)
                with pe.Fori(1, QUARTERS) as q:
                    up(q, 0)
                    down(q)

        A_X = A_R
        A_U = A_R + 41 * KB
        A_B = A_R + 121 * KB
        A_M = A_R + 161 * KB

        def both(name, chunks, at, dtype=F32):
            a = sb(name, [chunks, SEQ], at, dtype)
            return a, sb(name + "c", [chunks, CTX], at + chunks * SEQ * 4, dtype)

        def tile_of(pair, c, ti):
            return pair[0][:, c, TN * ti:TN * ti + TN] if ti < 2 else pair[1][:, c, :]

        def hl2(pairH, pairL):
            return lambda part, k, c0, n: tile_of(pairL if part else pairH, k, c0 // TN)

        x = (h, sb("xc", [KC, CTX], A_X + 32 * KB))
        u2H, u2L = both("u2H", KC, A_U, F32R), both("u2L", KC, A_U + 40 * KB, F32R)
        xs_d = nc.dram_tensor("x_scratch", (P, KC, SEQ), F32).ap()
        gates_d = nc.dram_tensor("gates_scratch", (KC, P, TOK), F32).ap()
        x2_d = nc.dram_tensor("x2_scratch", (P, KC, SEQ), F32).ap()
        ag_d = nc.dram_tensor("ag_scratch", (P, HALF, SEQ), F32).ap()

        def vec(ti):
            return 1 if ti == 2 else 0

        def mod_norm(name, layer, tmp, x_ready, squares=None):
            return Norm(name, lambda c, ti: tile_of(x, c, ti), TILES2,
                        lambda c, ti: gmod[:, layer, c, vec(ti):vec(ti) + 1],
                        lambda c, ti: modv[:, 24 * layer + c, vec(ti):vec(ti) + 1],
                        lambda part, c, ti: tile_of(u2L if part else u2H, c, ti), tmp, sum_banks=(6, 7, 5), x_ready=x_ready,
                        squares=squares)

        sig = sb("sig", [TOK], A_M)
        val = sb("val", [TOK], A_M + 5 * KB)
        bt = sb("bt", [TOK], A_M + 10 * KB)
        bf = sb("bf", [SEQ], A_M + 15 * KB)
        conv_in = sb("conv_in", [HALF, CONV_IN], A_X)
        CO_AT = A_X + (HALF * CONV_IN * 4 + 31) // 32 * 32
        conv_out = sb("conv_out", [HALF, CONV_OUT], CO_AT)
        bH = sb("bH", [HALF, TOK], A_B, F32R)
        bL = sb("bL", [HALF, TOK], A_B + 20 * KB, F32R)
        (ctx_loaded, x_spilled, mod_ready, mod_step, ein_done, ein_drained, ci_ready, ci_zero, conv_step,
         folded, fold_step, b_hi, b_lo) = (sem(v) for v in (
             "ctx_loaded x_spilled mod_ready mod_step ein_done ein_drained ci_ready ci_zero conv_step folded "
             "fold_step b_hi b_lo").split())
        gate_stored = [sem("gate_stored0"), sem("gate_stored1")]
        norm3 = Norm("norm3", lambda c, ti: h[:, c, TN * ti:TN * ti + TN], TILES1, lambda c, ti: pcol("final_norm", c),
                     None, None, A_M, out32=lambda c, ti: h[:, c, TN * ti:TN * ti + TN], sum_banks=(0, 1), squares=mlp_squares)

        def x_final(eng, c, ti):
            if ti < 2:
                norm3.wait(eng, "ready", ti * KC + c + 1)
            else:
                eng.wait_ge(ctx_loaded, 16)

        norm4 = mod_norm("norm4", 0, A_B, x_final)
        E0, T3 = W0["ein"], len(TILES2)
        MAIN0, CTX0 = PAD, PAD + SEQ + PAD
        CTX_OUT = SEQ + PAD
        E_FREE = 6
        with nc.Block() as block:
            @block.sync
            def _(sp):
                sp.dma_start(x[1][:], t["ctx"]).then_inc(ctx_loaded, 16)
                norm3.wait(sp, "ready", 2 * KC)
                sp.dma_start(xs_d, h[:]).then_inc(x_spilled, 16)
                loads(sp, "ein", "ein")

            @block.scalar
            def _(act):
                act.sem_inc(gate_stored[0], 16)
                act.sem_inc(gate_stored[1], 16)
                norm3.act(act)
                norm4.act(act)

                def drain(i, s, ti, dst, func):
                    j = (2 * i + s) * T3 + ti
                    act.wait_ge(ein_done, j + 1)
                    act.activation(dst, bank(s * T3 + ti, TILES2[ti][1]), func).then_inc(ein_drained, 1)

                with act.Fori(0, HALF) as i:
                    act.wait_ge(ci_ready, i + 1)
                    for s, (dst, func) in enumerate(((sig, ACT.Sigmoid), (val, ACT.Copy))):
                        for ti, (c0, n) in enumerate(TILES2):
                            drain(i, s, ti, dst[:, c0:c0 + n], func)
                with act.Fori(0, 2) as i:
                    for s in range(2):
                        act.wait_ge(b_lo, 2 * i + s + 1)
                        for ti, (c0, n) in enumerate(TILES2):
                            drain(i + 4, s, ti, bt[:, c0:c0 + n], ACT.Copy)
                        act.wait_ge(folded, 2 * i + s + 1)
                        g = bass.ds(2 * i + s, 1)
                        act.copy(bH[:, g, 0:SEQ].rearrange("p a n -> p (a n)"), bf[:]).then_inc(b_hi, 1)
                        act.copy(bH[:, g, SEQ:TOK].rearrange("p a n -> p (a n)"), bt[:, SEQ:TOK]).then_inc(b_hi, 1)
                act.wait_ge(ci_ready, HALF + 1)
                with act.Fori(0, 4) as i:
                    for s, buf in enumerate((sig, val)):
                        act.wait_ge(gate_stored[s], 16 * i + 16)
                        for ti, (c0, n) in enumerate(TILES2):
                            drain(i + 6, s, ti, buf[:, c0:c0 + n], ACT.Silu)
                        act.wait_ge(ein_drained, ((i + 6) * 2 + s) * T3 + T3 + E_FREE)
                        act.dma_start(gates_d[bass.ds(2 * i + s, 1)].rearrange("a p f -> p (a f)"), buf[:])\
                            .then_inc(gate_stored[s], 16)

            @block.gpsimd
            def _(pool):
                pool.sem_inc(ci_ready, 1)
                pool.sem_inc(b_lo, 1)
                split_unit(pool, E0 + 1, 0, 0)
                norm4.pool(pool)
                pool.wait_ge(x_spilled, 16)
                norm4.wait_ready(pool, 3 * KC)
                pool.memset(conv_in[:], 0.0).then_inc(ci_zero, 1)
                pool.wait_ge(ci_zero, 1)
                with pool.Fori(0, HALF) as i:
                    for s in range(2):
                        split_unit(pool, E0 + 2, i, s)
                    pool.wait_ge(ein_drained, (2 * i + 2) * T3 + E_FREE)
                    ci = conv_in[:, bass.ds(i, 1), :].rearrange("p a n -> p (a n)")
                    pool.tensor_tensor(ci[:, MAIN0:MAIN0 + SEQ], sig[:, 0:SEQ], val[:, 0:SEQ], ALU.mult)
                    pool.tensor_tensor(ci[:, CTX0:CTX0 + CTX], sig[:, SEQ:TOK], val[:, SEQ:TOK], ALU.mult)\
                        .then_inc(ci_ready, 1)
                with pool.Fori(0, 2) as i:
                    for s in range(2):
                        split_unit(pool, E0 + 10, i, s)
                        g = 2 * i + s
                        pool.wait_ge(ein_drained, (g + 9) * T3 + E_FREE)
                        pool.tensor_tensor(bf[:, 0:512], bt[:, 0:512], bt[:, 512:1024], ALU.subtract).then_inc(fold_step, 1)
                        pool.wait_ge(fold_step, 2 * g + 1)
                        pool.tensor_tensor(bt[:, 0:512], bt[:, 0:512], bt[:, 512:1024], ALU.add).then_inc(fold_step, 1)
                        pool.wait_ge(fold_step, 2 * g + 2)
                        pool.tensor_tensor(bf[:, 512:768], bt[:, 0:256], bt[:, 256:512], ALU.subtract)
                        pool.tensor_tensor(bf[:, 768:1024], bt[:, 0:256], bt[:, 256:512], ALU.add).then_inc(folded, 1)
                        pool.wait_ge(folded, g + 1)
                        pool.wait_ge(b_hi, 2 * g + 2)
                        gg = bass.ds(g, 1)
                        for o, src, n in ((0, bf[:], SEQ), (SEQ, bt[:, SEQ:TOK], CTX)):
                            m = pool.tensor_tensor(bL[:, gg, o:o + n].rearrange("p a n -> p (a n)"), src,
                                                   bH[:, gg, o:o + n].rearrange("p a n -> p (a n)").bitcast(F32), ALU.subtract)
                        m.then_inc(b_lo, 1)
                stream(pool, split_unit, E0 + 14, E0 + 21)

            @block.vector
            def _(dve):
                norm3.dve(dve)
                for v in range(2):
                    dve.tensor_tensor(modv[:, :, v], modv[:, :, v], par[:, PC["b_mod"]:PC["b_mod"] + 48], ALU.add)\
                        .then_inc(mod_step, 1)
                dve.wait_ge(mod_step, 2)
                for layer, name in enumerate(("e_norm", "o_norm")):
                    for v in range(2):
                        m = dve.scalar_tensor_tensor(gmod[:, layer, :, v], modv[:, 24 * layer + 8:24 * layer + 16, v], 1.0,
                                                     par[:, PC[name]:PC[name] + 8], ALU.add, ALU.mult)
                        m.then_inc(mod_ready, 1)
                dve.wait_ge(mod_ready, 4)
                norm3.wait(dve, "ready", 2 * KC)
                norm4.dve(dve)
                with dve.Fori(0, HALF) as c:
                    dve.wait_ge(ci_ready, c + 2)
                    for tap in range(TAPS):
                        src = conv_in[:, bass.ds(c, 1), tap:tap + CONV_OUT].rearrange("p a n -> p (a n)")
                        dst = conv_out[:, bass.ds(c, 1), :].rearrange("p a n -> p (a n)")
                        w = par[:, bass.ds(c * TAPS + (PC["conv_w"] + tap), 1)]
                        if tap == 0:
                            dve.tensor_scalar(dst, src, w, par[:, bass.ds(c + PC["conv_b"], 1)], ALU.mult, ALU.add)\
                                .then_inc(conv_step, 1)
                        else:
                            dve.wait_ge(conv_step, c * TAPS + tap)
                            dve.scalar_tensor_tensor(dst, src, w, dst, ALU.mult, ALU.add).then_inc(conv_step, 1)

            @block.tensor
            def _(pe):
                pe.sem_inc(units_begun, 1)
                norm3.pe(pe)
                norm4.pe(pe)
                linear(pe, E0, 20, TILES2, hl2(u2H, u2L), ein_done, ein_drained, norm4)

        LN_SQ = 4
        ZC = 10
        zH = sb("zH", [ZC, D], A_U, F32R)
        zL = sb("zL", [ZC, D], A_U + 40 * KB, F32R)
        sH = sb("sH", [HALF, CONV_OUT], A_X, F32R)
        sL = sb("sL", [HALF, CONV_OUT], CO_AT, F32R)
        sq = sb("ln_sq", [LN_SQ, TN], A_M)
        rs = sb("ln_rs", [TOK], A_M + 8 * KB)
        STILES = [(0, TN), (TN, TN), (CTX_OUT, CTX)]
        (sum_done, centred, ln_sq_ready, ln_sq_used, ln_rms, ln_rstd, ln_v, ln_silu, s_hi, s_lo, z_done, z_hi,
         z_lo) = (sem("ln_" + v) for v in "sum_done centred sq_ready sq_used rms rstd v silu s_hi s_lo z_done z_hi z_lo".split())
        Z_BANKS, MEAN_BANKS = (6, 0), (2, 5, 4)
        jobs = [(ti, c) for ti in range(3) for c in range(HALF)]
        fH = sb("fH", [HALF, TOK], A_B, F32R)
        fL = sb("fL", [HALF, TOK], A_B + 20 * KB, F32R)
        yH, yL = both("yH", KC, A_U, F32R), both("yL", KC, A_U + 40 * KB, F32R)
        gt = sb("gt", [2, TOK], A_M + 19 * KB)
        gv = sb("gv", [3, TN], A_M + 13 * KB)
        (dft_done, f_hi, f_lo, mix_done, mix_v, y_hi, y_lo) = (sem(v) for v in
                                                               "dft_done f_hi f_lo mix_done mix_v y_hi y_lo".split())
        gate_loaded = [sem("gate_loaded0"), sem("gate_loaded1")]
        ODD, MOD2, MOD0 = (6, 7, 2, 0), (4, 5), (1, 3)
        def strided(r, m):
            return lambda f, g: f[:, g, 0:SEQ].rearrange("p (n m) -> p n m", m=m)[:, :, r]
        fjobs = [(ODD[g], 0, 512, g, strided(1, 2), 1.0) for g in range(4)]
        fjobs += [(MOD2[g // 2], 256 * (g % 2), 256, g, strided(2, 4), 1.0) for g in range(4)]
        fjobs += [(MOD0[g // 2], 256 * (g % 2), 256, g, strided(0, 4), 1.0) for g in range(4)]
        fjobs += [(MOD2[g // 2], 256 * (g % 2), 256, g, lambda f, g: f[:, g, SEQ:TOK], 2.0) for g in range(4)]
        mjobs = [(4 + g, 4 + g, None, ti) for g in range(4) for ti in range(3)] + \
                [(f, f, pcol("pw_b", f), ti) for f in range(4) for ti in range(3)]
        with nc.Block() as block:
            @block.sync
            def _(sp):
                order = [4, 5, 6, 7, 0, 1, 2, 3]
                for s in range(2):
                    sp.wait_ge(gate_stored[s], 16 * 5)
                for i, g in enumerate(order):
                    if i == 2:
                        loads(sp, "dft", "dft")
                    if i >= 2:
                        sp.wait_ge(mix_v, 3 * (i - 1))
                    sp.dma_start(gt[:, i % 2, :], gates_d[g]).then_inc(gate_loaded[i % 2], 16)
                loads(sp, "fw", "pw")

            @block.gpsimd
            def _(pool):
                splits(pool, "dft", "pw")

            @block.tensor
            def _(pe):
                for ti, (c0, n) in enumerate(STILES):
                    for c in range(HALF):
                        m = pe.matmul(bank(MEAN_BANKS[ti], n), ones[:], conv_out[:, c, c0:c0 + n], start=c == 0, stop=c == HALF - 1)
                    m.then_inc(sum_done, 1)
                def square_sum(j):
                    ti, c = jobs[j]
                    if j == HALF:
                        pe.wait_ge(centred, len(jobs))
                    pe.wait_ge(ln_sq_ready, j + 1)
                    pe.matmul(bank(3 + ti, TILES2[ti][1]), ones[:], sq[:, j % LN_SQ, 0:TILES2[ti][1]], start=c == 0,
                              stop=c == HALF - 1).then_inc(ln_sq_used, 1)

                for z in range(ZC):
                    if z >= 2:
                        pe.wait_ge(z_lo, 2 * (z - 1))
                    for g in range(HALF):
                        w = slice(z * P, z * P + P)
                        _, m = mm3(pe, banks[:, Z_BANKS[z % 2] + g // 2, (g % 2) * 256:(g % 2) * 256 + 256],
                                   bH[:, g, w], bL[:, g, w], cdsH[:], cdsL[:], True, True)
                        if g % 2:
                            m.then_inc(z_done, 1)
                    if z >= 1:
                        square_sum(z - 1)
                for j in range(ZC - 1, len(jobs)):
                    square_sum(j)
                pe.wait_ge(z_lo, 2 * (ZC - 1))

                def begin(u):
                    pe.wait_ge(weights_split, u + 1 + W_FREE)
                    return u % 2
                D0 = W0["dft"]
                for tc in range(4):
                    slot = begin(D0 + tc)
                    for g in range(HALF):
                        if tc == 0 and g == 3:
                            pe.wait_ge(z_lo, 2 * ZC)
                        for part in range(2):
                            zw = slice(g * 256 + part * P, g * 256 + part * P + P)
                            ww = slice(part * 512, part * 512 + 512)
                            f, m = mm3(pe, bank(ODD[g]), zH[:, tc, zw], zL[:, tc, zw], wH[:, slot, ww], wL[:, slot, ww],
                                       tc == 0 and part == 0, tc == 3 and part == 1)
                            if g == 0 and part == 0:
                                f.then_inc(units_begun, 1)
                        if tc == 3:
                            m.then_inc(dft_done, 1)
                for half in range(3):
                    u = D0 + 4 + min(half, 1)
                    slot = begin(u) if half < 2 else u % 2
                    if half == 0:
                        pe.wait_ge(ln_rms, 3)
                    if half == 2:
                        pe.wait_ge(f_lo, 8)
                    for g in range(HALF):
                        for tc in range(2):
                            for part in range(2):
                                zw = slice(g * 256 + part * P, g * 256 + part * P + P)
                                ww = slice(tc * 512 + part * 256, tc * 512 + part * 256 + 256)
                                b = (MOD2, MOD0, MOD2)[half][g // 2]
                                f, m = mm3(pe, banks[:, b, 256 * (g % 2):256 * (g % 2) + 256], zH[:, 4 + 2 * half + tc, zw],
                                           zL[:, 4 + 2 * half + tc, zw], wH[:, slot, ww], wL[:, slot, ww],
                                           tc == 0 and part == 0, tc == 1 and part == 1)
                                if g == 0 and tc == 0 and part == 0 and half < 2:
                                    f.then_inc(units_begun, 1)
                        m.then_inc(dft_done, 1)
                for j, (_, _, bias, ti) in enumerate(mjobs):
                    oc, (c0, n) = j // 3, TILES2[ti]
                    if oc < 4:
                        u, blocks, rhs = W0["fw"], [oc], lambda part, k, g=oc: (fL if part else fH)[:, g, c0:c0 + n]
                    else:
                        o, m_ = STILES[ti]
                        u, blocks = W0["pw"] + (oc - 4) // 2, [4 * (oc % 2) + k for k in range(4)]
                        rhs = lambda part, k: (sL if part else sH)[:, k, o:o + m_]
                    slot = begin(u)
                    if oc == 4 and ti == 0:
                        pe.wait_ge(s_lo, len(jobs))
                    if j < 6:
                        pe.wait_ge(f_lo, 16)
                    else:
                        pe.wait_ge(mix_v, j - 5)
                    for k, blk in enumerate(blocks):
                        w = slice(blk * P, blk * P + P)
                        f, m = mm3(pe, bank(j % 6, n), wH[:, slot, w], wL[:, slot, w], rhs(0, k), rhs(1, k), k == 0,
                                   k == len(blocks) - 1)
                        if k == 0 and ti == 0 and oc in (0, 4, 6):
                            f.then_inc(units_begun, 1)
                    m.then_inc(mix_done, 1)

            @block.scalar
            def _(act):
                def square(j):
                    ti, c = jobs[j]
                    c0, n = STILES[ti]
                    act.wait_ge(centred, j + 1)
                    if j >= LN_SQ:
                        act.wait_ge(ln_sq_used, j - LN_SQ + 1)
                    act.activation(sq[:, j % LN_SQ, 0:n], conv_out[:, c, c0:c0 + n], ACT.Square).then_inc(ln_sq_ready, 1)

                for s in range(2):
                    act.wait_ge(gate_stored[s], 16 * 5)
                for j in range(LN_SQ):
                    square(j)
                for z in range(ZC):
                    for half in range(2):
                        act.wait_ge(z_done, 2 * z + half + 1)
                        act.copy(zH[:, z, TN * half:TN * half + TN], bank(Z_BANKS[z % 2] + half)).then_inc(z_hi, 1)
                    if z >= 1 and z - 1 + LN_SQ < len(jobs):
                        square(z - 1 + LN_SQ)
                for ti, (c0, n) in enumerate(STILES):
                    act.wait_ge(ln_sq_used, (ti + 1) * HALF)
                    act.activation(rs[:, TILES2[ti][0]:TILES2[ti][0] + n], bank(3 + ti, n), ACT.Sqrt, bias=eps[:, 0:1], scale=1.0 / 512)\
                        .then_inc(ln_rms, 1)
                for j, (ti, c) in enumerate(jobs):
                    c0, n = STILES[ti]
                    v = conv_out[:, c, c0:c0 + n]
                    act.wait_ge(ln_v, j + 1)
                    act.activation(v, v, ACT.Silu, bias=pcol("ln_b", c)).then_inc(ln_silu, 1)
                    act.wait_ge(ln_silu, j + 1)
                    act.copy(sH[:, c, c0:c0 + n], v).then_inc(s_hi, 1)
                for j, (b, o, n, g, dst, scale) in enumerate(fjobs):
                    act.wait_ge(dft_done, j + 1 if j < 4 or g % 2 else j + 2)
                    if j >= 4 and g % 2:
                        act.wait_ge(f_lo, j)
                    act.activation(dst(fH, g), banks[:, b, o:o + n], ACT.Copy, scale=scale).then_inc(f_hi, 1)
                for j, (yc, gc, bias, ti) in enumerate(mjobs):
                    act.wait_ge(mix_v, j + 1)
                    act.copy(tile_of(yH, yc, ti), gv[:, j % 3, 0:TILES2[ti][1]]).then_inc(y_hi, 1)

            @block.vector
            def _(dve):
                for j, (ti, c) in enumerate(jobs):
                    c0, n = STILES[ti]
                    dve.wait_ge(sum_done, ti + 1)
                    v = conv_out[:, c, c0:c0 + n]
                    dve.scalar_tensor_tensor(v, bank(MEAN_BANKS[ti], n), -1.0 / 512, v, ALU.mult, ALU.add).then_inc(centred, 1)
                for z in range(2 * ZC):
                    dve.wait_ge(z_hi, z + 1)
                    w = slice(TN * (z % 2), TN * (z % 2) + TN)
                    dve.tensor_tensor(zL[:, z // 2, w], bank(Z_BANKS[z // 2 % 2] + z % 2), zH[:, z // 2, w].bitcast(F32),
                                      ALU.subtract).then_inc(z_lo, 1)
                for ti, (c0, n) in enumerate(STILES):
                    dve.wait_ge(ln_rms, ti + 1)
                    dve.reciprocal(rs[:, TILES2[ti][0]:TILES2[ti][0] + n], rs[:, TILES2[ti][0]:TILES2[ti][0] + n]).then_inc(ln_rstd, 1)
                    dve.wait_ge(ln_rstd, ti + 1)
                    for c in range(HALF):
                        v = conv_out[:, c, c0:c0 + n]
                        dve.scalar_tensor_tensor(v, v, pcol("ln_g", c), rs[:, TILES2[ti][0]:TILES2[ti][0] + n], ALU.mult, ALU.mult).then_inc(ln_v, 1)
                for j, (ti, c) in enumerate(jobs):
                    c0, n = STILES[ti]
                    dve.wait_ge(s_hi, j + 1)
                    dve.tensor_tensor(sL[:, c, c0:c0 + n], conv_out[:, c, c0:c0 + n], sH[:, c, c0:c0 + n].bitcast(F32),
                                      ALU.subtract).then_inc(s_lo, 1)
                for j, (b, o, n, g, dst, scale) in enumerate(fjobs):
                    dve.wait_ge(f_hi, j + 1)
                    dve.scalar_tensor_tensor(dst(fL, g), banks[:, b, o:o + n], scale, dst(fH, g).bitcast(F32), ALU.mult,
                                             ALU.subtract).then_inc(f_lo, 1)

                def low(j):
                    yc, gc, bias, ti = mjobs[j]
                    dve.wait_ge(y_hi, j + 1)
                    dve.tensor_tensor(tile_of(yL, yc, ti), gv[:, j % 3, 0:TILES2[ti][1]],
                                      tile_of(yH, yc, ti).bitcast(F32), ALU.subtract).then_inc(y_lo, 1)

                for j, (yc, gc, bias, ti) in enumerate(mjobs):
                    c0, n = TILES2[ti]
                    dve.wait_ge(mix_done, j + 1)
                    dve.wait_ge(gate_loaded[j // 3 % 2], 16 * (j // 6 + 1))
                    if j >= 3:
                        dve.wait_ge(y_lo, j - 2)
                    g = gt[:, j // 3 % 2, c0:c0 + n]
                    if bias is None:
                        dve.tensor_tensor(gv[:, j % 3, 0:n], bank(j % 6, n), g, ALU.mult).then_inc(mix_v, 1)
                    else:
                        dve.scalar_tensor_tensor(gv[:, j % 3, 0:n], bank(j % 6, n), bias, g, ALU.add, ALU.mult)\
                            .then_inc(mix_v, 1)
                    if j >= 1:
                        low(j - 1)
                low(len(mjobs) - 1)

        eout_done, eout_drained = sem("eout_done"), sem("eout_drained")
        x_back = sem("x_back")
        eout_squares = Squares("eout_squares", TILES2, A_B)
        with nc.Block() as block:
            @block.sync
            def _(sp):
                sp.dma_start(h[:], xs_d).then_inc(x_back, 16)
                sp.dma_start(x[1][:], t["ctx"]).then_inc(x_back, 16)
                loads(sp, "eout", "eout")

            @block.gpsimd
            def _(pool):
                splits(pool, "eout", "eout")

            @block.scalar
            def _(act):
                with act.Fori(0, 4) as i:
                    for s in range(2):
                        for ti, (c0, n) in enumerate(TILES2):
                            j = (2 * i + s) * T3 + ti
                            act.wait_ge(eout_drained, j + 1 + 2 * T3)
                            f = bass.ds(2 * i + s, 1)
                            src = (h[:, f, c0:c0 + n] if ti < 2 else x[1][:, f, :]).rearrange("p a n -> p (a n)")
                            eout_squares.act(act, j, (s * T3 + ti) % 2, src, n)

            @block.vector
            def _(dve):
                eout_squares.start(dve)
                dve.wait_ge(x_back, 32)
                with dve.Fori(0, 4) as i:
                    for s in range(2):
                        for ti, (c0, n) in enumerate(TILES2):
                            dve.wait_ge(eout_done, (2 * i + s) * T3 + ti + 1)
                            f = bass.ds(2 * i + s, 1)
                            dst = (h[:, f, c0:c0 + n] if ti < 2 else x[1][:, f, :]).rearrange("p a n -> p (a n)")
                            g = modv[:, bass.ds(2 * i + (16 + s), 1), vec(ti):vec(ti) + 1].rearrange("p a n -> p (a n)")
                            dve.scalar_tensor_tensor(dst, bank(s * T3 + ti, n), g, dst, ALU.mult, ALU.add)\
                                .then_inc(eout_drained, 1)
                            eout_squares.dve(dve, (2 * i + s) * T3 + ti, (s * T3 + ti) % 2, ti, n)

            @block.tensor
            def _(pe):
                linear(pe, W0["eout"], 8, TILES2, hl2(yH, yL), eout_done, eout_drained)

        qH = sb("qH", [HALF, SEQ], A_B, F32R)
        qL = sb("qL", [HALF, SEQ], A_B + 16 * KB, F32R)
        k2H = sb("k2H", [TOK], A_B + 32 * KB, F32R)
        mask = sb("mask", [3 * P], A_B + 37 * KB)
        zeros = sb("zeros", [2 * P], A_B + 37 * KB + 1536)
        ycH = sb("ycH", [HALF, SEQ], A_X, F32R)
        ycL = sb("ycL", [HALF, SEQ], A_X + 16 * KB, F32R)
        k2L = sb("k2L", [TOK], A_X + 32 * KB, F32R)
        rope = sb("rope", [2, SEQ], A_M)
        rt = sb("rt", [2, TN], A_M + 8 * KB)
        rr = sb("rr", [2, TN], A_M + 12 * KB)
        rv = sb("rv", [2, TN], A_M + 16 * KB)
        v2T = sb("v2T", [TOK], A_M + 20 * KB)
        ag = sb("ag", [SEQ], A_M + 25 * KB)
        SPARE = A_U + 40 * KB + 32 * KB
        prod = sb("prod", [SEQ + 2], A_M)
        cc = sb("cc", [SEQ], A_M + 5 * KB)
        cv = sb("cv", [SEQ], A_M + 9 * KB)
        cs = sb("cs", [2, TN], A_M + 13 * KB)
        cw = sb("cw", [2, TN], SPARE)
        O0 = W0["oin"]
        names = ("x2_spilled rope_loaded kv_done k_drained rt_ready rot_done rr_ready rot_v q_hi q_lo q_done kc_hi "
                 "ag_done ag_drained ag_stored cc_done cc_drained cx_done cx_drained cb_done cb_drained cg_done cg_drained "
                 "c_step c_v yc_hi yc_lo prod_zero rt_used").split()
        S = {v: sem("o_" + v) for v in names}
        norm5 = mod_norm("norm5", 1, A_M, None, eout_squares)
        with nc.Block() as block:
            @block.sync
            def _(sp):
                sp.dma_start(x2_d, h[:]).then_inc(S["x2_spilled"], 16)
                sp.dma_start(mask[:], t["mask"]).then_inc(S["rope_loaded"], 16)
                norm5.wait_ready(sp, 3 * KC)
                sp.dma_start(rope[:], t["rope"]).then_inc(S["rope_loaded"], 16)
                loads(sp, "oin", "oin")

            @block.gpsimd
            def _(pool):
                split_unit(pool, O0 + 1, 0, 0)
                norm5.pool(pool)
                splits(pool, "oin", "oin", 2)

            def rotate_pe(pe, n0, ti, granted=0):
                j = n0 + ti
                pe.wait_ge(S["rt_ready"], j + 1 + granted)
                pe.wait_ge(S["rr_ready"], j + 1)
                pe.matmul(bank(6 + ti), swap[:], rt[:, ti, :], start=True, stop=True).then_inc(S["rot_done"], 1)

            @block.tensor
            def _(pe):
                pe.sem_inc(units_begun, 1)
                norm5.pe(pe)
                pe.sem_inc(S["k_drained"], 6)
                pe.sem_inc(S["rr_ready"], 2)
                first_pair(pe, O0, TILES2, hl2(u2H, u2L), lambda s, ti: s * T3 + ti, S["kv_done"], norm5)
                pe.wait_ge(S["k_drained"], 6 + 4)
                pe.sem_inc(S["rt_ready"], 4)
                with pe.Fori(0, 2) as i:
                    for s in range(2):
                        linear_unit(pe, O0 + 2, i, s, (2 * i + s) * 2, KC, TILES1, hl2(u2H, u2L),
                                    lambda s, ti: s * 2 + ti, S["q_done"], S["rt_ready"], off=2)
                        for ti in range(2):
                            rotate_pe(pe, (2 * i + s) * 2, ti, 4)
                pe.wait_ge(S["rt_ready"], 4 + 8)
                pe.sem_inc(S["ag_drained"], 4)
                for n in range(4):
                    i, s = divmod(n, 2)
                    linear_unit(pe, O0 + 6, i, s, 2 * n, KC, TILES1, hl2(u2H, u2L),
                                lambda s, ti: s * 2 + ti, S["ag_done"], S["ag_drained"])
                    if n == 0:
                        for ti in range(2):
                            rotate_pe(pe, 8, ti, 4)
                pe.wait_ge(S["ag_drained"], 12)
                pe.wait_ge(S["rr_ready"], 12)
                for v in ("cc", "cx", "cb", "cg"):
                    pe.sem_inc(S[v + "_drained"], 2)
                with pe.Fori(0, 4) as i:
                    for y, v in enumerate(("cc", "cx", "cb", "cg")):
                        linear_unit(pe, O0 + 10 + y, 2 * i, 0, 2 * i, KC, TILES1, hl2(u2H, u2L),
                                    lambda s, ti, y=y: 2 * y + ti, S[v + "_done"], S[v + "_drained"])

            @block.scalar
            def _(act):
                norm5.act(act)
                norm5.wait_ready(act, 3 * KC)

                def rot_in(n0, ti, done, at, b):
                    j = n0 + ti
                    act.wait_ge(done, at)
                    if not (isinstance(j, int) and j < 2):
                        act.wait_ge(S["rot_v"], j - 1)
                    act.copy(rt[:, ti, :], bank(b)).then_inc(S["rt_ready"], 1)

                def rot_hi(n0, ti, dst):
                    act.wait_ge(S["rot_v"], n0 + ti + 1)
                    act.copy(dst, rv[:, ti, :]).then_inc(S["q_hi"], 1)

                for ti in range(2):
                    rot_in(0, ti, S["kv_done"], ti + 1, ti)
                act.wait_ge(S["kv_done"], 3)
                act.copy(k2H[:, SEQ:TOK], bank(2, CTX)).then_inc(S["kc_hi"], 1)
                for ti, (c0, n) in enumerate(TILES2):
                    act.wait_ge(S["kv_done"], 4 + ti)
                    act.copy(v2T[:, c0:c0 + n], bank(3 + ti, n)).then_inc(S["k_drained"], 1)
                for ti in range(2):
                    rot_hi(0, ti, k2H[:, TN * ti:TN * ti + TN])
                with act.Fori(0, 2) as i:
                    for s in range(2):
                        n0 = 2 + (2 * i + s) * 2
                        for ti in range(2):
                            rot_in(n0, ti, S["q_done"], (2 * i + s) * 2 + ti + 1, s * 2 + ti)
                        for ti in range(2):
                            rot_hi(n0, ti, qH[:, bass.ds(2 * i + s, 1), TN * ti:TN * ti + TN].rearrange("p a n -> p (a n)"))
                act.sem_inc(S["ag_stored"], 16)
                with act.Fori(0, 2) as i:
                    for s in range(2):
                        act.wait_ge(S["ag_stored"], (2 * i + s + 1) * 16)
                        for ti in range(2):
                            act.wait_ge(S["ag_done"], (2 * i + s) * 2 + ti + 1)
                            act.activation(ag[:, TN * ti:TN * ti + TN], bank(s * 2 + ti), ACT.Silu).then_inc(S["ag_drained"], 1)
                        act.wait_ge(S["ag_drained"], (2 * i + s) * 2 + 2 + 4)
                        act.dma_start(ag_d[:, bass.ds(2 * i + s, 1), :].rearrange("p a n -> p (a n)"), ag[:])\
                            .then_inc(S["ag_stored"], 16)
                act.wait_ge(S["q_lo"], 10)
                with act.Fori(0, 4) as i:
                    for ti in range(2):
                        act.wait_ge(S["cc_done"], 2 * i + ti + 1)
                        act.wait_ge(S["cx_drained"], 2 * i + 2)
                        act.copy(cc[:, TN * ti:TN * ti + TN], bank(ti)).then_inc(S["cc_drained"], 1)
                    for ti in range(2):
                        act.wait_ge(S["cg_done"], 2 * i + ti + 1)
                        act.wait_ge(S["c_v"], 2 * i + ti + 1)
                        act.activation(cs[:, ti, :], bank(6 + ti), ACT.Silu).then_inc(S["cg_drained"], 1)
                    for ti in range(2):
                        act.wait_ge(S["c_v"], 2 * i + ti + 3)
                        act.copy(ycH[:, bass.ds(i, 1), TN * ti:TN * ti + TN].rearrange("p a n -> p (a n)"), cw[:, ti, :])\
                            .then_inc(S["yc_hi"], 1)

            @block.vector
            def _(dve):
                dve.memset(zeros[:], 0.0)
                norm5.dve(dve)
                dve.wait_ge(S["rope_loaded"], 32)
                norm5.wait_ready(dve, 3 * KC)

                def rot(n0, ti):
                    j = n0 + ti
                    w = slice(TN * ti, TN * ti + TN)
                    dve.wait_ge(S["rot_done"], j + 1)
                    if not (isinstance(j, int) and j < 2):
                        dve.wait_ge(S["q_lo"], j - 1)
                    dve.tensor_tensor(rr[:, ti, :], bank(6 + ti), rope[:, 1, w], ALU.mult).then_inc(S["rr_ready"], 1)
                    dve.tensor_tensor(rt[:, ti, :], rt[:, ti, :], rope[:, 0, w], ALU.mult).then_inc(S["rt_used"], 1)
                    dve.wait_ge(S["rt_used"], j + 1)
                    dve.wait_ge(S["rr_ready"], j + 3)
                    dve.tensor_tensor(rv[:, ti, :], rt[:, ti, :], rr[:, ti, :], ALU.add).then_inc(S["rot_v"], 1)

                def rot_lo(n0, ti, H, L):
                    dve.wait_ge(S["q_hi"], n0 + ti + 1)
                    dve.tensor_tensor(L, rv[:, ti, :], H.bitcast(F32), ALU.subtract).then_inc(S["q_lo"], 1)

                dve.wait_ge(S["kc_hi"], 1)
                dve.tensor_tensor(k2L[:, SEQ:TOK], bank(2, CTX), k2H[:, SEQ:TOK].bitcast(F32), ALU.subtract)\
                    .then_inc(S["k_drained"], 1)
                for ti in range(2):
                    rot(0, ti)
                for ti in range(2):
                    rot_lo(0, ti, k2H[:, TN * ti:TN * ti + TN], k2L[:, TN * ti:TN * ti + TN])
                with dve.Fori(0, 2) as i:
                    for s in range(2):
                        n0 = 2 + (2 * i + s) * 2
                        for ti in range(2):
                            rot(n0, ti)
                        for ti in range(2):
                            H, L = (a[:, bass.ds(2 * i + s, 1), TN * ti:TN * ti + TN].rearrange("p a n -> p (a n)")
                                    for a in (qH, qL))
                            rot_lo(n0, ti, H, L)
                dve.wait_ge(S["x2_spilled"], 16)
                dve.wait_ge(S["q_lo"], 10)
                dve.sem_inc(S["c_v"], 2)
                for edge in (0, SEQ + 1):
                    dve.memset(prod[:, edge:edge + 1], 0.0).then_inc(S["prod_zero"], 1)
                dve.wait_ge(S["prod_zero"], 2)
                with dve.Fori(0, 4) as i:
                    for ti in range(2):
                        dve.wait_ge(S["cx_done"], 2 * i + ti + 1)
                        dve.wait_ge(S["cc_drained"], 2 * i + ti + 3)
                        dve.wait_ge(S["cx_drained"], 2 * i + 2)
                        dve.tensor_tensor(prod[:, 1 + TN * ti:1 + TN * ti + TN], bank(2 + ti), cc[:, TN * ti:TN * ti + TN],
                                          ALU.mult).then_inc(S["cx_drained"], 1)
                    dve.wait_ge(S["cx_drained"], 2 * i + 4)
                    for tap in range(3):
                        w = par[:, bass.ds(3 * i + (PC["c_conv_w"] + tap), 1)]
                        if tap == 0:
                            dve.tensor_scalar(cv[:], prod[:, 0:SEQ], w, None, ALU.mult).then_inc(S["c_step"], 1)
                        else:
                            dve.wait_ge(S["c_step"], 3 * i + tap)
                            dve.scalar_tensor_tensor(cv[:], prod[:, tap:tap + SEQ], w, cv[:], ALU.mult, ALU.add)\
                                .then_inc(S["c_step"], 1)
                    dve.wait_ge(S["c_step"], 3 * i + 3)
                    for ti in range(2):
                        c = cv[:, TN * ti:TN * ti + TN]
                        dve.wait_ge(S["cb_done"], 2 * i + ti + 1)
                        dve.tensor_tensor(c, bank(4 + ti), c, ALU.mult).then_inc(S["cb_drained"], 1)
                    for ti in range(2):
                        dve.wait_ge(S["cb_drained"], 2 * i + ti + 3)
                        dve.wait_ge(S["cg_drained"], 2 * i + ti + 3)
                        dve.tensor_tensor(cw[:, ti, :], cv[:, TN * ti:TN * ti + TN], cs[:, ti, :], ALU.mult).then_inc(S["c_v"], 1)
                    for ti in range(2):
                        H, L = (a[:, bass.ds(i, 1), TN * ti:TN * ti + TN].rearrange("p a n -> p (a n)") for a in (ycH, ycL))
                        dve.wait_ge(S["yc_hi"], 2 * i + ti + 1)
                        dve.tensor_tensor(L, cw[:, ti, :], H.bitcast(F32), ALU.subtract).then_inc(S["yc_lo"], 1)
                    dve.wait_ge(S["yc_lo"], 2 * i + 2)

        vz2H = sb("vz2H", [10, 2, P], A_M, F32R)
        vz2L = sb("vz2L", [10, 2, P], A_M + 10 * KB, F32R)
        gate_tile = sb("gate_tile", [2, HALF, P], A_M + 25 * KB)
        gated_out = sb("gated_out", [HALF, P], A_X + 37 * KB)
        ag_loaded = [sem("ag_loaded0"), sem("ag_loaded1")]

        def span(n):
            return max(n - 1, 0), min(n + 2, NB)

        def s_tiles2(st):
            n, _ = st
            lo, hi = span(n)
            w = (hi - lo) * P
            out = []
            for c2 in (0, 2):
                for ci in (c2, c2 + 1):
                    for kv in range(2):
                        out.append([(2 * ci + kv, kv, ci, lo * P, w, 384 - w, 0)])
                for kv in range(2):
                    out.append([(2 * ci + kv, kv, ci, SEQ, CTX, 384, CTX * (ci % 2)) for ci in (c2, c2 + 1)])
            return out

        def t_tiles2(st):
            lo, hi = span(st[0])
            w = (hi - lo) * P
            cols = [(b, 384 - w + (b - lo) * P) for b in range(lo, hi)] + [(NB + b, 384 + b * P) for b in range(2)]
            return [(kv, b, col) for kv in range(2) for b, col in cols]

        def in1_2(head, off, w, st):
            n = st[0]
            m0 = (span(n)[0] - (n - 1)) * P
            return zeros[:, 0:w] if off >= 384 else mask[:, m0:m0 + w]

        attention("win", [(n, 0) for n in range(NB)], s_tiles2, t_tiles2, 8, 640, qH, qL, k2H, k2L, vz2H, vz2L, in1_2,
                  lambda head: 16 + head, A_U, A_U + 60 * KB, 5,
                  gate={"tmp": gated_out[:], "tile": lambda i: gate_tile[:, i], "loaded": ag_loaded,
                    "stored": (S["ag_stored"], 5 * 16),
                        "source": lambda n: ag_d[:, :, n * P:n * P + P]},
                  vsrc=v2T, vblocks=10, chain_max=True)

        xo = sb("xo", [KC, SEQ], A_U)
        oout_done, oout_drained, xo_scaled, stored = sem("oout_done"), sem("oout_drained"), sem("xo_scaled"), sem("stored")
        oout_squares = Squares("oout_squares", TILES1, A_U + 40 * KB)
        norm6 = Norm("norm6", lambda c, ti: xo[:, c, TN * ti:TN * ti + TN], TILES1, None, None, None, A_M,
                     out32=lambda c, ti: xo[:, c, TN * ti:TN * ti + TN], sum_banks=(4, 5), squares=oout_squares,
                     scaled=True)
        with nc.Block() as block:
            @block.sync
            def _(sp):
                sp.dma_start(xo[:], x2_d).then_inc(x_back, 16)
                loads(sp, "oout", "oout")
                for ti in range(2):
                    for c in range(KC):
                        norm6.wait_ready(sp, ti * KC + c + 1)
                        sp.dma_start(t["out"][:, c, TN * ti:TN * ti + TN], xo[:, c, TN * ti:TN * ti + TN]).then_inc(stored, 16)
                sp.wait_ge(stored, 16 * 2 * KC)

            @block.gpsimd
            def _(pool):
                splits(pool, "oout", "oout")
                pool.wait_ge(xo_scaled, 2 * KC)
                norm6.pool(pool)

            @block.vector
            def _(dve):
                oout_squares.start(dve)
                dve.wait_ge(x_back, 32 + 16)
                with dve.Fori(0, 4) as i:
                    for s in range(2):
                        for ti in range(2):
                            dve.wait_ge(oout_done, (2 * i + s) * 2 + ti + 1)
                            dst = xo[:, bass.ds(2 * i + s, 1), TN * ti:TN * ti + TN].rearrange("p a n -> p (a n)")
                            g = modv[:, bass.ds(2 * i + (40 + s), 1), 0:1].rearrange("p a n -> p (a n)")
                            dve.scalar_tensor_tensor(dst, bank(s * 2 + ti), g, dst, ALU.mult, ALU.add)\
                                .then_inc(oout_drained, 1)
                            oout_squares.dve(dve, (2 * i + s) * 2 + ti, ti, ti, TN)
                dve.wait_ge(xo_scaled, 2 * KC)
                norm6.dve(dve)

            @block.scalar
            def _(act):
                with act.Fori(0, 4) as i:
                    for s in range(2):
                        for ti in range(2):
                            j = (2 * i + s) * 2 + ti
                            c = xo[:, bass.ds(2 * i + s, 1), TN * ti:TN * ti + TN].rearrange("p a n -> p (a n)")
                            act.wait_ge(oout_drained, j + 1 + 4)
                            oout_squares.act(act, j, ti, c, TN)
                            act.activation(c, c, ACT.Copy, scale=par[:, bass.ds(2 * i + (PC["final_norm2"] + s), 1)])\
                                .then_inc(xo_scaled, 1)
                norm6.act(act)

            @block.tensor
            def _(pe):
                linear(pe, W0["oout"], 8, TILES1,
                       lambda part, k, c0, n: ((ycL if part else ycH)[:, k, c0:c0 + n] if k < HALF else
                                               (qL if part else qH)[:, k - HALF, c0:c0 + n]), oout_done, oout_drained)
                norm6.pe(pe)


def constants():
    import numpy as np
    f = np.float32
    k = {}
    k["ident"] = np.eye(P, dtype=f)
    sw = np.zeros((P, P), f)
    for i in range(P):
        sw[i ^ 16, i] = 1.0
    k["swap"] = sw
    th = 2 * np.pi * (np.outer(np.arange(P), np.arange(P)) % P) / P
    k["cds"] = (np.concatenate([np.cos(th), np.sin(th)], 1) / np.sqrt(P)).astype(f)
    dist = P + np.arange(P)[:, None] - np.arange(2 * P)[None, :]
    slopes = np.exp2(-8.0 * np.arange(1, 17, dtype=f) / 16).astype(f)
    b = -slopes[None, :, None] * dist[:, None, :].astype(f)
    b = np.where(((dist >= 0) & (dist < P))[:, None, :], b, f(-1e30))
    k["bias8"] = (b * f(8)).astype(f)
    dist = P + np.arange(P)[:, None] - np.arange(3 * P)[None, :]
    k["mask"] = np.where(np.abs(dist) <= P, f(0), f(-8e30)).astype(f)
    inv = np.power(f(10000.0), -np.arange(16, dtype=f) / f(16)).astype(f)
    tok = np.arange(SEQ)
    feat = np.arange(P) % 64
    pos = np.where((feat < 32)[:, None], (tok // 64)[None], (tok % 64)[None]).astype(f)
    ang = (pos * inv[feat % 16][:, None]).astype(f)
    sign = np.where(feat % 32 < 16, f(-1), f(1))[:, None]
    k["rope"] = np.stack([np.cos(ang), np.sin(ang) * sign], 1).astype(f)
    return k


def pack_units(w):
    K, F = w.shape
    return w.reshape(K // P, P, F // P, P).transpose(2, 1, 0, 3).reshape(F // P, P, K)


def chunked(v):
    return v.reshape(-1, P, *v.shape[1:]).swapaxes(0, 1)


def head_order(kv_group):
    import numpy as np
    return np.array([(kv * kv_group + c) * 64 + d for c in range(kv_group) for kv in range(2) for d in range(64)])


def layout(a):
    import numpy as np
    f = np.float32
    o8, o4 = head_order(8), head_order(4)
    wq = a["swa_w_qkv"][0]
    units = [pack_units(np.concatenate([wq[:, :1024][:, o8], wq[:, 1024:]], 1)), pack_units(a["swa_w_o"][0][o8])]
    up, down = pack_units(a["mlp_w_up"][0]), a["mlp_w_down"][0]
    for q in range(4):
        units += [up[8 * q:8 * q + 8], pack_units(down[D * q:D * q + D])]
    ein = pack_units(a["e_w_in_2"][0])
    for i in range(4):
        units += [ein[4 + i:5 + i], ein[i:i + 1]]
    units += [ein[12:16], ein[8:12], ein[16:20]]
    def dft(tt, ll):
        th = 2 * np.pi * (np.outer(tt, ll) % SEQ) / SEQ
        return np.concatenate([np.cos(th), -np.sin(th)], 1).astype(f) / f(32)
    for tc in range(4):
        units.append(dft(np.arange(tc * P, tc * P + P), 2 * np.arange(512) + 1)[None])
    for r in (2, 0):
        units.append(np.concatenate([dft(np.arange(tc * P, tc * P + P), 4 * np.arange(256) + r) for tc in range(2)], 1)[None])
    fw = a["e_b_fw_2"][0].transpose(1, 0, 2).reshape(P, 512)
    units.append(np.concatenate([fw, np.zeros((P, 512), f)], 1)[None])
    pw = pack_units(a["e_a_pw_w_2"][0])
    units.append(pw.reshape(2, 2, P, 512).transpose(0, 2, 1, 3).reshape(2, P, 1024))
    units.append(pack_units(a["e_w_out_2"][0]))
    oi = a["o_w_in_2"][0]
    q = pack_units(oi[:, 2048:2560][:, o4])
    ag = pack_units(oi[:, 2816:][:, o4])
    rest = pack_units(oi[:, :2816])
    units += [rest[20:22], q, ag]
    for i in range(4):
        units += [rest[4 + i:5 + i], rest[8 + i:9 + i], rest[i:i + 1], rest[12 + i:13 + i]]
    wo2 = a["o_w_out_2"][0]
    units.append(pack_units(np.concatenate([wo2[:512], wo2[512:][o4]], 0)))
    out = {"wstream": np.concatenate(units, 0)}
    assert out["wstream"].shape == (UNITS, P, D), out["wstream"].shape
    out["x"] = chunked(a["x"][0].T)
    rep = lambda v: np.broadcast_to(v[None], (P, *v.shape))
    cols = [chunked(a["attn_norm"][0]), chunked(a["mlp_norm"][0]), chunked(a["final_norm"]), chunked(a["e_norm_2"][0]),
            chunked(a["o_norm_2"][0]), chunked(a["final_norm_2"]), chunked(a["e_b_mod_2"][0]), chunked(a["o_b_mod_2"][0]),
            chunked(a["e_a_conv_w_2"][0].T).reshape(P, -1), chunked(a["e_a_conv_b_2"][0]), chunked(a["e_a_ln_g_2"][0]),
            chunked(a["e_a_ln_b_2"][0]), chunked(a["e_a_pw_b_2"][0]), chunked(a["o_c_conv_w_2"][0].T).reshape(P, -1),
            rep(a["swa_sinks"][0]), rep(a["o_sink_2"][0])]
    out["par"] = np.concatenate(cols, 1)
    assert out["par"].shape == (P, NPAR)
    out["mod_w"] = np.concatenate([a["e_w_mod_2"][0].T.reshape(24, P, D), a["o_w_mod_2"][0].T.reshape(24, P, D)], 0)
    out["cvec"] = np.broadcast_to(np.stack([a["c_2"][0], a["c_ctx_2"]])[None], (P, 2, D))
    out["ctx"] = chunked(a["ctx_2"][0].T)
    out.update(constants())
    return {k: np.ascontiguousarray(v) for k, v in out.items()}


def kernel(**inputs):
    import numpy as np
    import concourse.bacc as bacc
    from concourse.bass_utils import run_bass_kernel_spmd as run

    nc = bacc.Bacc("TRN2", target_bir_lowering=False, num_devices=1, dynamic_dma_scratch_size=1024)
    arrays = layout({k: np.asarray(v) for k, v in inputs.items()})
    t = {k: nc.dram_tensor("in_" + k, v.shape, mybir.dt.from_np(v.dtype), kind="ExternalInput").ap() for k, v in arrays.items()}
    t["out"] = nc.dram_tensor("out_y", (P, KC, SEQ), F32, kind="ExternalOutput").ap()
    build(nc, t)
    r = run(nc, [{"in_" + k: v for k, v in arrays.items()}], core_ids=[0])
    y = r.results[0]["out_y"]
    return y.transpose(2, 1, 0).reshape(1, SEQ, D)
```
